# Optimizing a Trainium2 kernel written in Bass

```python
import jax, jax.numpy as jnp
from jax import lax
import numpy as np

D_MODEL = 1024
BATCH = 1
SEQ = 256
DEPTH = 2
DEC_BATCH = 8
DEC_SEQ = 8
PAST_LEN = 2048
PAGE_SIZE = 128

HEAD_DIM = 64
N_HEADS = 8
N_KV_HEADS = 2
GROUP = N_HEADS // N_KV_HEADS
ATTN_DIM = N_HEADS * HEAD_DIM
KV_DIM = N_KV_HEADS * HEAD_DIM
WINDOW = 128
ATTN_SCALE = HEAD_DIM ** -0.5
CONV_DIM = 256
CONV_WIDTH = 3
N_MEM = 256
MEM_HEADS = 4
MEM_DIM = MEM_HEADS * HEAD_DIM
N_BRANCH = 3
IN_DIM = ATTN_DIM + 2 * KV_DIM + 3 * CONV_DIM + MEM_DIM + N_BRANCH * D_MODEL
D_FF = 2816
N_EXPERTS = 8
TOP_K = 2
N_DENSE = (DEPTH + 1) // 2
N_MOE = DEPTH // 2
ALPHA = (2 * DEPTH) ** 0.25
BETA = (8 * DEPTH) ** -0.25
LN_EPS = 1e-5

kernel_name = "hybrid_swa_sink_shortconv_memxattn_moe_deepnorm_step"

def _layer_norm(x, g, b):
    xf = x.astype(jnp.float32)
    mu = jnp.mean(xf, axis=-1, keepdims=True)
    var = jnp.mean(jnp.square(xf - mu), axis=-1, keepdims=True)
    y = (xf - mu) * lax.rsqrt(var + LN_EPS) * g.astype(jnp.float32) + b.astype(jnp.float32)
    return y.astype(x.dtype)

def _split_in(z):
    sizes = (ATTN_DIM, KV_DIM, KV_DIM, CONV_DIM, CONV_DIM, CONV_DIM, MEM_DIM,
             D_MODEL, D_MODEL, D_MODEL)
    idx = np.cumsum(sizes)[:-1].tolist()
    return jnp.split(z, idx, axis=-1)

def _sink_softmax(s, sink):
    m = jnp.maximum(jnp.max(s, axis=-1, keepdims=True), sink)
    e = jnp.exp(s - m)
    return e / (jnp.sum(e, axis=-1, keepdims=True) + jnp.exp(sink - m))

def _window_attn_prompt(q, k, v, sink):
    b, s = q.shape[:2]
    nb = s // WINDOW
    qb = q.reshape(b, nb, WINDOW, N_KV_HEADS, GROUP, HEAD_DIM)
    kb = k.reshape(b, nb, WINDOW, N_KV_HEADS, HEAD_DIM)
    vb = v.reshape(b, nb, WINDOW, N_KV_HEADS, HEAD_DIM)

    def band(t):
        prev = jnp.concatenate([jnp.zeros_like(t[:, :1]), t[:, :-1]], axis=1)
        return jnp.concatenate([prev, t], axis=2)

    kband, vband = band(kb), band(vb)
    sc = jnp.einsum('bnqkgd,bnjkd->bnkgqj', qb, kband,
                    preferred_element_type=jnp.float32) * ATTN_SCALE
    qi = jnp.arange(WINDOW)[:, None]
    kj = jnp.arange(2 * WINDOW)[None, :]
    dist = qi + WINDOW - kj
    kpos = jnp.arange(nb)[:, None, None] * WINDOW + kj - WINDOW
    mask = (dist >= 0) & (dist < WINDOW) & (kpos >= 0)
    sc = jnp.where(mask[:, None, None], sc, -jnp.inf)
    p = _sink_softmax(sc, sink.astype(jnp.float32).reshape(N_KV_HEADS, GROUP, 1, 1))
    o = jnp.einsum('bnkgqj,bnjkd->bnqkgd', p.astype(v.dtype), vband)
    tail = min(WINDOW, s)
    return o.reshape(b, s, ATTN_DIM), k[:, s - tail:], v[:, s - tail:]

def _window_attn_sample(q, k, v, buf_k, buf_v, sink):
    b, t = q.shape[:2]
    nbuf = buf_k.shape[1]
    k_all = jnp.concatenate([buf_k, k], axis=1)
    v_all = jnp.concatenate([buf_v, v], axis=1)
    qg = q.reshape(b, t, N_KV_HEADS, GROUP, HEAD_DIM)
    sc = jnp.einsum('btkgd,bjkd->bkgtj', qg, k_all,
                    preferred_element_type=jnp.float32) * ATTN_SCALE
    dist = jnp.arange(t)[:, None] + nbuf - jnp.arange(nbuf + t)[None, :]
    mask = (dist >= 0) & (dist < WINDOW)
    sc = jnp.where(mask, sc, -jnp.inf)
    p = _sink_softmax(sc, sink.astype(jnp.float32).reshape(N_KV_HEADS, GROUP, 1, 1))
    o = jnp.einsum('bkgtj,bjkd->btkgd', p.astype(v.dtype), v_all)
    return o.reshape(b, t, ATTN_DIM), k_all[:, t:], v_all[:, t:]

def _short_conv(u_ext, w):
    t = u_ext.shape[1] - (CONV_WIDTH - 1)
    out = w[0] * u_ext[:, 0:t]
    for j in range(1, CONV_WIDTH):
        out = out + w[j] * u_ext[:, j:j + t]
    return out

def _mem_attn(qm, km, vm):
    sc = jnp.einsum('bshd,bmhd->bhsm', qm, km, preferred_element_type=jnp.float32) * ATTN_SCALE
    p = jax.nn.softmax(sc, axis=-1)
    o = jnp.einsum('bhsm,bmhd->bshd', p.astype(vm.dtype), vm)
    return o.reshape(qm.shape[0], qm.shape[1], MEM_DIM)

def _mixer(x, w_in, conv_w, sink, p_attn, p_conv, p_mem, w_o, mem_k, mem_v,
           buf_k, buf_v, buf_conv):
    b, t = x.shape[:2]
    q, k, v, h, g_b, g_c, qm, gate_a, gate_c, gate_m = _split_in(x @ w_in)
    q = q.reshape(b, t, N_HEADS, HEAD_DIM)
    k = k.reshape(b, t, N_KV_HEADS, HEAD_DIM)
    v = v.reshape(b, t, N_KV_HEADS, HEAD_DIM)
    if buf_k is None:
        o_a, nk, nv = _window_attn_prompt(q, k, v, sink)
        u_prev = jnp.zeros((b, CONV_WIDTH - 1, CONV_DIM), x.dtype)
    else:
        o_a, nk, nv = _window_attn_sample(q, k, v, buf_k, buf_v, sink)
        u_prev = buf_conv
    u_ext = jnp.concatenate([u_prev, g_c * h], axis=1)
    o_c = g_b * _short_conv(u_ext, conv_w)
    o_m = _mem_attn(qm.reshape(b, t, MEM_HEADS, HEAD_DIM), mem_k, mem_v)
    merged = (jax.nn.sigmoid(gate_a) * (o_a @ p_attn)
              + jax.nn.sigmoid(gate_c) * (o_c @ p_conv)
              + jax.nn.sigmoid(gate_m) * (o_m @ p_mem))
    new_conv = u_ext[:, u_ext.shape[1] - (CONV_WIDTH - 1):]
    return merged @ w_o, nk, nv, new_conv

def _swiglu(x, wg, wu, wd):
    return (jax.nn.silu(x @ wg) * (x @ wu)) @ wd

def _moe(x, w_router, b_router, wg, wu, wd):
    shp = x.shape
    xt = x.reshape(-1, D_MODEL)
    logits = jnp.dot(xt, w_router, preferred_element_type=jnp.float32) + b_router.astype(jnp.float32)
    top_v, top_i = lax.top_k(logits, TOP_K)
    top_w = jax.nn.softmax(top_v, axis=-1)
    gates = jnp.sum(jax.nn.one_hot(top_i, N_EXPERTS, dtype=jnp.float32) * top_w[..., None], axis=1)
    gates = gates.astype(x.dtype)
    y = jnp.zeros_like(xt)
    for e in range(N_EXPERTS):
        y = y + gates[:, e:e + 1] * _swiglu(xt, wg[e], wu[e], wd[e])
    return y.reshape(shp)

def _ffn(x, l, ffn_w_gate, ffn_w_up, ffn_w_down, router_w, router_b,
         exp_w_gate, exp_w_up, exp_w_down):
    i = l // 2
    if l % 2 == 0:
        return _swiglu(x, ffn_w_gate[i], ffn_w_up[i], ffn_w_down[i])
    return _moe(x, router_w[i], router_b[i], exp_w_gate[i], exp_w_up[i], exp_w_down[i])

def setup_inputs(seed: int = 0) -> dict:
    key = jax.random.key(seed)
    ks = jax.random.split(key, 32)
    f32 = jnp.float32

    def nrm(k, shape, scale):
        return jax.random.normal(k, shape, f32) * scale

    win_buf = min(WINDOW, PAST_LEN)
    return {
        "x_prompt": nrm(ks[0], (BATCH, SEQ, D_MODEL), 1.0),
        "x_sample": nrm(ks[1], (DEC_BATCH, DEC_SEQ, D_MODEL), 1.0),
        "mem_prompt": nrm(ks[2], (BATCH, N_MEM, D_MODEL), 1.0),
        "cache_win_k": nrm(ks[3], (DEPTH, DEC_BATCH, win_buf, N_KV_HEADS, HEAD_DIM), 1.0),
        "cache_win_v": nrm(ks[4], (DEPTH, DEC_BATCH, win_buf, N_KV_HEADS, HEAD_DIM), 1.0),
        "cache_conv": nrm(ks[5], (DEPTH, DEC_BATCH, CONV_WIDTH - 1, CONV_DIM), 1.0),
        "cache_mem_k": nrm(ks[6], (DEPTH, DEC_BATCH, N_MEM, MEM_HEADS, HEAD_DIM), 1.0),
        "cache_mem_v": nrm(ks[7], (DEPTH, DEC_BATCH, N_MEM, MEM_HEADS, HEAD_DIM), 1.0),
        "w_in": nrm(ks[8], (DEPTH, D_MODEL, IN_DIM), D_MODEL ** -0.5),
        "conv_w": nrm(ks[9], (DEPTH, CONV_WIDTH, CONV_DIM), CONV_WIDTH ** -0.5),
        "sink": nrm(ks[10], (DEPTH, N_HEADS), 1.0),
        "p_attn": nrm(ks[11], (DEPTH, ATTN_DIM, D_MODEL), ATTN_DIM ** -0.5),
        "p_conv": nrm(ks[12], (DEPTH, CONV_DIM, D_MODEL), CONV_DIM ** -0.5),
        "p_mem": nrm(ks[13], (DEPTH, MEM_DIM, D_MODEL), MEM_DIM ** -0.5),
        "w_o": nrm(ks[14], (DEPTH, D_MODEL, D_MODEL), BETA * D_MODEL ** -0.5),
        "w_mem_k": nrm(ks[15], (DEPTH, D_MODEL, MEM_DIM), D_MODEL ** -0.5),
        "w_mem_v": nrm(ks[16], (DEPTH, D_MODEL, MEM_DIM), D_MODEL ** -0.5),
        "ln1_g": 1.0 + nrm(ks[17], (DEPTH, D_MODEL), 0.02),
        "ln1_b": nrm(ks[18], (DEPTH, D_MODEL), 0.02),
        "ln2_g": 1.0 + nrm(ks[19], (DEPTH, D_MODEL), 0.02),
        "ln2_b": nrm(ks[20], (DEPTH, D_MODEL), 0.02),
        "ffn_w_gate": nrm(ks[21], (N_DENSE, D_MODEL, D_FF), D_MODEL ** -0.5),
        "ffn_w_up": nrm(ks[22], (N_DENSE, D_MODEL, D_FF), D_MODEL ** -0.5),
        "ffn_w_down": nrm(ks[23], (N_DENSE, D_FF, D_MODEL), BETA * D_FF ** -0.5),
        "router_w": nrm(ks[24], (N_MOE, D_MODEL, N_EXPERTS), D_MODEL ** -0.5),
        "router_b": nrm(ks[25], (N_MOE, N_EXPERTS), 0.01),
        "exp_w_gate": nrm(ks[26], (N_MOE, N_EXPERTS, D_MODEL, D_FF), D_MODEL ** -0.5),
        "exp_w_up": nrm(ks[27], (N_MOE, N_EXPERTS, D_MODEL, D_FF), D_MODEL ** -0.5),
        "exp_w_down": nrm(ks[28], (N_MOE, N_EXPERTS, D_FF, D_MODEL), BETA * D_FF ** -0.5),
    }

def reference(x_prompt, x_sample, mem_prompt, cache_win_k, cache_win_v, cache_conv,
              cache_mem_k, cache_mem_v, w_in, conv_w, sink, p_attn, p_conv, p_mem, w_o,
              w_mem_k, w_mem_v, ln1_g, ln1_b, ln2_g, ln2_b, ffn_w_gate, ffn_w_up,
              ffn_w_down, router_w, router_b, exp_w_gate, exp_w_up, exp_w_down):
    xp, xs = x_prompt, x_sample
    wk_p, wv_p, cv_p, mk_p, mv_p, wk_s, wv_s, cv_s = [], [], [], [], [], [], [], []
    b, n_mem = mem_prompt.shape[:2]
    for l in range(DEPTH):
        mk = (mem_prompt @ w_mem_k[l]).reshape(b, n_mem, MEM_HEADS, HEAD_DIM)
        mv = (mem_prompt @ w_mem_v[l]).reshape(b, n_mem, MEM_HEADS, HEAD_DIM)
        mix, nk, nv, nc = _mixer(xp, w_in[l], conv_w[l], sink[l], p_attn[l], p_conv[l],
                                 p_mem[l], w_o[l], mk, mv, None, None, None)
        xp = _layer_norm(ALPHA * xp + mix, ln1_g[l], ln1_b[l])
        xp = _layer_norm(ALPHA * xp + _ffn(xp, l, ffn_w_gate, ffn_w_up, ffn_w_down, router_w,
                                           router_b, exp_w_gate, exp_w_up, exp_w_down),
                         ln2_g[l], ln2_b[l])
        wk_p.append(nk); wv_p.append(nv); cv_p.append(nc); mk_p.append(mk); mv_p.append(mv)
        mix, nk, nv, nc = _mixer(xs, w_in[l], conv_w[l], sink[l], p_attn[l], p_conv[l],
                                 p_mem[l], w_o[l], cache_mem_k[l], cache_mem_v[l],
                                 cache_win_k[l], cache_win_v[l], cache_conv[l])
        xs = _layer_norm(ALPHA * xs + mix, ln1_g[l], ln1_b[l])
        xs = _layer_norm(ALPHA * xs + _ffn(xs, l, ffn_w_gate, ffn_w_up, ffn_w_down, router_w,
                                           router_b, exp_w_gate, exp_w_up, exp_w_down),
                         ln2_g[l], ln2_b[l])
        wk_s.append(nk); wv_s.append(nv); cv_s.append(nc)
    return (xp, xs, jnp.stack(wk_p), jnp.stack(wv_p), jnp.stack(cv_p), jnp.stack(mk_p),
            jnp.stack(mv_p), jnp.stack(wk_s), jnp.stack(wv_s), jnp.stack(cv_s))


_drawn_inputs = setup_inputs


def setup_inputs(seed=0):
    import zlib

    import numpy as np

    out = dict(_drawn_inputs(seed))
    spreads = {}
    factors = {'sink': 8.0, 'router_b': 4.855}
    for name, (base, spread) in spreads.items():
        noise = np.random.default_rng([zlib.crc32(name.encode()), seed]).standard_normal(out[name].shape)
        drawn = base * np.exp(spread * noise) if base else spread * noise
        out[name] = __import__('jax').numpy.asarray(drawn.astype(out[name].dtype))
    for name, factor in factors.items():
        out[name] = (out[name] * factor).astype(out[name].dtype)
    return out
```

```python
from contextlib import ExitStack

import concourse.bass as bass
from concourse import mybir

F32 = mybir.dt.float32
F32R = mybir.dt.float32r
I32 = mybir.dt.int32
U32 = mybir.dt.uint32
ALU = mybir.AluOpType
ACT = mybir.ActivationFunctionType
AX = mybir.AxisListType.X

P = 128
D = 1024
KD = D // P
NP = 256
NB = 8
TS = 8
NS = NB * TS
T = NP + NS
HD = 64
NEG = -1.0e30
SCALE = HD ** -0.5
ALPHA = 4 ** 0.25
EPS = 1e-5
FF = 2816
NBLK = FF // 256
NE = 8
ROUNDS = 3

UNIT = 2048
RING = 6
HI_RING = 3
RING_MOE = 11
AHEAD = HI_RING - 1

FIN_BANK = (0, 1, 2, 3, 6, 7)
TILES = ((0, 128), (128, 128), (256, 64))

Z_COLS = ([1536, 0, 256, 512, 768, 1024, 1280]
          + [2816 + 256 * i for i in range(4)]
          + [3840 + 256 * i for i in range(4)]
          + [1792 + 256 * i for i in range(4)])


def layer_units(l):
    z = [("z", l, i) for i in range(19)]
    return (z[0:11] + [("pconv", l, 0)] + z[11:15] + [("pmem", l, 0)] + z[15:19]
            + [("pattn", l, i) for i in range(2)] + [("wo", l, i) for i in range(4)])


def ffn_units():
    return [(k, 0, i) for i in range(NBLK) for k in ("fg", "fu")] + [("fd", 0, i) for i in range(NBLK)]


STREAM = ([(k, l, 0) for l in range(2) for k in ("mk", "mv")]
          + layer_units(0) + ffn_units() + layer_units(1))
N_DENSE = len(STREAM)
UNIT_OF = {u: n for n, u in enumerate(STREAM)}
EXPERT = [("a", 0), ("b", 0)]
for _i in range(1, NBLK):
    EXPERT += [("a", _i), ("b", _i), ("d", _i - 1)]
EXPERT += [("d", NBLK - 1)]
NX = len(EXPERT)
assert NX % RING_MOE == 0 and NX % HI_RING == 0
LDX_VALUE, _at = [], [0] * RING_MOE
for _n, (_k, _) in enumerate(EXPERT):
    _at[_n % RING_MOE] += 16 if _k == "d" else 32
    LDX_VALUE.append(_at[_n % RING_MOE])
LDX_STEP = list(_at)
SIDE = {EXPERT.index(u): ("scatter", (2 * c, 2 * c + 1))
        for c, u in enumerate((("b", 0), ("a", 1), ("b", 1), ("a", 2)))}
SIDE.update({EXPERT.index(("b", NBLK - 6 + c)): ("gather", c) for c in range(4)})
SIDE[EXPERT.index(("b", NBLK - 2))] = ("slots", 0)

LD_VALUE, _at = [], [0] * RING_MOE
for _n, _u in enumerate(STREAM):
    _at[_n % RING] += 32 if _u[0] == "pattn" else 16
    LD_VALUE.append(_at[_n % RING])
LD_BASE = list(_at)

JOBS = [("pmem", 0), ("pmem", 1), ("smem", 0), ("smem", 1),
        ("pwin", (0, 0)), ("pwin", (0, 1)), ("pwin", (1, 0)), ("pwin", (1, 1)), ("swin", 0)]
NJ = len(JOBS)
SEGMENT_HEADS = (0, 2, 1, 3)


def job_shape(kind, idx):
    if kind == "smem":
        return 1, 256
    if kind == "pmem":
        return 4, 256
    if kind == "pwin":
        return 4, 128 * (idx[0] + 1)
    return 4, 192


def beside_units():
    after = {0: [("event", "memk", 0, 0)], 1: [], 3: []}
    for j in range(NJ):
        for lag, work in ((0, ("scores", j)), (2, ("event", "probs", j, 0)), (3, ("pv", j))):
            after.setdefault(2 * j + lag, []).append(work)
    after[1].append(("event", "memk", 0, 1))
    after[4] += [("event", "kvtok", 0, 0), ("event", "memk", 1, 0)]
    after[5].append(("event", "memk", 1, 1))
    after[8].append(("event", "wink", 0, 0))
    after[9].append(("event", "conv", 0, 0))
    order = {"pv": 0, "event": 1, "scores": 2}
    for w in after:
        after[w].sort(key=lambda x: 3 if x[0] == "event" and x[1] != "probs" else order[x[0]])
    return after


SLOTS = beside_units()
EVENTS = [x[1:] for w in sorted(SLOTS) for x in SLOTS[w] if x[0] == "event"]
N_EVENTS = len(EVENTS)
EVENT_NO = {e: n for n, e in enumerate(EVENTS)}

OUTS = []
for _u in layer_units(0):
    if _u[0] == "z":
        OUTS += [("z", 2 * _u[2]), ("z", 2 * _u[2] + 1)]
    elif _u[0] in ("pconv", "pmem"):
        OUTS += [(_u[0], f) for f in range(KD)]
    elif _u[0] == "pattn":
        OUTS += [("pattn", 4 * _u[2] + f) for f in range(4)]
    else:
        OUTS += [("wo", 2 * _u[2]), ("wo", 2 * _u[2] + 1)]
OUT_NO = {o: n for n, o in enumerate(OUTS)}
OUT_SIGNAL, _mid = {}, 0
for _k, _u in enumerate(layer_units(0)):
    _n = {"z": 2, "wo": 2, "pattn": 4, "pconv": KD, "pmem": KD}[_u[0]]
    for _m in range(_n):
        _mid += _m < _n - 1
        OUT_SIGNAL[OUTS[len(OUT_SIGNAL)]] = (_k, _m == _n - 1, _mid)
OUT_MIDS = _mid
MERGES = [o for o in OUTS if o[0] in ("pconv", "pmem", "pattn")]
MERGE_NO = {o: n for n, o in enumerate(MERGES)}


def build_trunk(nc, A, O):
    with ExitStack() as ctx:
        base = (nc.sbuf_base + 63) // 64 * 64
        end = nc.sbuf_usable_end
        place = {"at": base}

        def at(name, shape, dt, offset):
            words = 1
            for s in shape[1:]:
                words *= s
            assert offset + 4 * words <= end, (name, offset + 4 * words - end)
            return nc.alloc_sbuf_tensor_at(name, shape, dt, offset=offset)

        def take(name, shape, dt=F32):
            words = 1
            for s in shape[1:]:
                words *= s
            t = at(name, shape, dt, place["at"])
            place["at"] += (4 * words + 31) // 32 * 32
            return t

        def sem(name):
            return ctx.enter_context(nc.semaphore(name))

        ring_at = place["at"]
        raw = [at(f"raw{s}", [P, UNIT], F32, ring_at + 4 * UNIT * s) for s in range(RING)]
        low = [at(f"low{s}", [P, UNIT], F32R, ring_at + 4 * UNIT * s) for s in range(RING)]
        place["at"] = ring_at + 4 * UNIT * RING
        high = [take(f"high{s}", [P, UNIT], F32R) for s in range(HI_RING)]

        x = take("x", [P, KD, T])
        ident = take("ident", [P, P])
        mean_of = take("mean_of", [P, P])
        mask_win = take("mask_win", [P, 256])
        mask_dec = take("mask_dec", [P, 2, 192])
        vecs = take("vecs", [P, 76])
        sink_p = take("sink_p", [P, 2, 8])
        sink_s = take("sink_s", [P, 2, 2])
        small = take("small", [P, 64])
        eps = take("eps", [P, 1])
        std = take("std", [P, T])
        iota_i = at("iota_i", [P, P], I32, place["at"] - 4 * T)
        ulast = take("ulast", [P, 2, 18])
        uout = take("uout", [18, 256])
        iota_f = take("iota_f", [P, P])
        row_i = take("row_i", [P, 4], I32)
        row_f = take("row_f", [P, 4])
        scratch_at = place["at"]

        xh = take("xh", [P, KD, T], F32R)
        xl = take("xl", [P, KD, T], F32R)
        mkT = take("mkT", [P, 2, 2, 256])
        mv = take("mv", [P, 2, 2, 256])
        mix_at = place["at"]
        gate = take("gate", [P, KD, T])
        sq_dense = at("sq_dense", [P, KD, T], F32, mix_at)
        merged = take("merged", [P, KD, T])
        hbc = at("hbc", [P, 6, T], F32, place["at"] - 4 * KD * T)
        qT = take("qT", [P, 4, NP])
        qS = take("qS", [P, NB, 4, TS])
        qmT = take("qmT", [P, 2, NP])
        qm_diag = take("qm_diag", [P, 2, NB, 32])
        kvT = take("kvT", [P, 2, T])
        uext = take("uext", [P, 2, NP + 2 + NB * (TS + 2)])
        sc = take("sc", [P, 4, 256])
        pT = take("pT", [P, 2, 512])
        oah = take("oah", [P, 4, T], F32R)
        oal = take("oal", [P, 4, T], F32R)
        omh = take("omh", [P, 2, T], F32R)
        oml = take("oml", [P, 2, T], F32R)
        och = take("och", [P, 2, T], F32R)
        ocl = take("ocl", [P, 2, T], F32R)
        kvtok = take("kvtok", [P, 2, 3, P])
        kstage = take("kstage", [P, 4, 2, 256])
        mem_kT_at = place["at"]
        mem_kT = take("mem_kT", [P, 4, 2, 256])
        win_kT = at("win_kT", [P, NB, P], F32, mem_kT_at)
        win_v = at("win_v", [P, NB, P], F32, mem_kT_at + 4096)
        mem_v = take("mem_v", [P, 4, 2, 256])
        ustage = at("ustage", [16, 256], F32, mix_at + 4 * 14 * T)
        wstage = at("wstage", [P, NB, P], F32, place["at"] - 4 * 3 * 2048)

        xstage = at("xstage", [P, 3, D], F32, mix_at)
        mstage = at("mstage", [P, 2, D], F32, mix_at + 12288)
        mTh = at("mTh", [P, KD, NP], F32R, mix_at + 20480)
        mTl = at("mTl", [P, KD, NP], F32R, mix_at + 28672)
        mtok = at("mtok", [P, 2, 2, 256], F32, mix_at + 36864)
        vstage = at("vstage", [76, P], F32, mix_at + 40960)

        hTh = at("hTh", [P, 22, T], F32R, mix_at)
        hTl = at("hTl", [P, 22, T], F32R, mix_at + 4 * 22 * T)
        silu = at("silu", [P, 2, 2, T], F32, mix_at + 8 * 22 * T)
        hfull = at("hfull", [P, 2, 2, T], F32, mix_at + 8 * 22 * T + 16 * T)

        place["at"] = scratch_at
        xtokh = take("xtokh", [P, 3, D], F32R)
        xtokl = take("xtokl", [P, 3, D], F32R)
        xeh = take("xeh", [P, KD, P], F32R)
        xel = take("xel", [P, KD, P], F32R)
        xnh = take("xnh", [P, KD, P], F32R)
        xnl = take("xnl", [P, KD, P], F32R)
        ygh = take("ygh", [P, D], F32R)
        ygl = take("ygl", [P, D], F32R)
        sil = take("sil", [P, 2, 256])
        hf = take("hf", [P, 2, 256])
        heh = take("heh", [P, 2, 2, P], F32R)
        hel = take("hel", [P, 2, 2, P], F32R)
        onehot = take("onehot", [P, 3, P], F32R)
        slot_next = take("slot_next", [P, T], F32R)
        slot_cur = take("slot_cur", [P, T], F32R)
        gs_next = take("gs_next", [P, 1])
        gs_cur = take("gs_cur", [P, 1])
        gcol = take("gcol", [P, 3])
        rw = take("rw", [P, KD, NE])
        rb = take("rb", [P, NE])
        logit = take("logit", [P, 3, NE])
        top = take("top", [P, 3, 8])
        topi = take("topi", [P, 3, 8], U32)
        topf = take("topf", [P, 3, 8])
        pair = take("pair", [P, 3, 4])
        oh1 = take("oh1", [P, 3, NE])
        oh2 = take("oh2", [P, 3, NE])
        chosen = take("chosen", [P, 3, NE])
        gates = take("gates", [P, 3, ROUNDS * NE + 1])
        posm = take("posm", [P, 3, NE])
        pos = take("pos", [P, 3, ROUNDS * NE + 1])
        before = take("before", [P, P])
        ones = take("ones", [P, P])
        cnt = take("cnt", [P, 4])
        total_i = take("total_i", [P, 1], I32)
        sq_last = take("sq_last", [P, KD, T])
        yout = at("yout", [P, 3, D], F32, scratch_at)
        ext_at = end - 4 * UNIT * (RING_MOE - RING)
        ext_at -= ext_at % 64
        assert place["at"] <= ext_at, place["at"] - ext_at
        raw_moe = raw + [at(f"raw{s}", [P, UNIT], F32, ext_at + 4 * UNIT * (s - RING))
                         for s in range(RING, RING_MOE)]
        low_moe = low + [at(f"low{s}", [P, UNIT], F32R, ext_at + 4 * UNIT * (s - RING))
                         for s in range(RING, RING_MOE)]

        ps = ctx.enter_context(nc.psum_tensor("ps", [P, 8, 512], F32))
        ps_sc = ps[:, 4:6, :].rearrange("p b (s w) -> p (b s) w", w=256)
        ps_tr = ps[:, 6:8, :]
        MEAN, VAR = 4, 5

        ld = [sem(f"loaded{s}") for s in range(RING_MOE)]
        hi_done = sem("hi_done")
        lo_done = sem("lo_done")
        unit_done = sem("unit_done")
        zeroed = sem("zeroed")
        slot_ok = sem("slot_ok")
        ld_x = sem("ld_x")
        ld_mem = sem("ld_mem")
        ld_vec = sem("ld_vec")
        ld_const = sem("ld_const")
        const = sem("const")
        vconst = sem("vconst")
        start_tr = sem("start_tr")
        start_hi = sem("start_hi")
        start_lo = sem("start_lo")
        mem_cp = sem("mem_cp")
        mkT_tr = sem("mkT_tr")
        mkT_cp = sem("mkT_cp")
        out_mm = sem("out_mm")
        z_cp = sem("z_cp")
        conv_done = sem("conv_done")
        och_done = sem("och_done")
        ocl_done = sem("ocl_done")
        merge_done = sem("merge_done")
        mh_done = sem("mh_done")
        ml_done = sem("ml_done")
        sc_mm = sem("sc_mm")
        sc_cp = sem("sc_cp")
        exp_done = sem("exp_done")
        probs = sem("probs")
        tr_mm = sem("tr_mm")
        tr_cp = sem("tr_cp")
        pv_mm = sem("pv_mm")
        o_hi = sem("o_hi")
        o_lo = sem("o_lo")
        ulast_done = sem("ulast_done")
        ld_memk = sem("ld_memk")
        ld_memv = sem("ld_memv")
        ld_wink = sem("ld_wink")
        ld_winv = sem("ld_winv")
        ld_conv = sem("ld_conv")
        resid = sem("resid")
        mean_mm = sem("mean_mm")
        centered = sem("centered")
        squared = sem("squared")
        var_mm = sem("var_mm")
        std_done = sem("std_done")
        rstd_done = sem("rstd_done")
        normed = sem("normed")
        xh_done = sem("xh_done")
        x_done = sem("x_done")
        xl_done = sem("xl_done")
        ff_silu = sem("ff_silu")
        ff_h = sem("ff_h")
        ff_hi = sem("ff_hi")
        ff_lo = sem("ff_lo")
        down_mm = sem("down_mm")
        rt_mm = sem("rt_mm")
        rt_top = sem("rt_top")
        rt_exp = sem("rt_exp")
        rt_sel = sem("rt_sel")
        rt_rank = sem("rt_rank")
        rt_total = sem("rt_total")
        xt_mm = sem("xt_mm")
        xt_hi = sem("xt_hi")
        xt_lo = sem("xt_lo")
        oh_done = sem("oh_done")
        side_mm = sem("side_mm")
        side_cp = sem("side_cp")
        xe_ok = sem("xe_ok")
        xel_ok = sem("xel_ok")
        xe_hi = sem("xe_hi")
        e_silu = sem("e_silu")
        e_h = sem("e_h")
        e_tr = sem("e_tr")
        e_hi = sem("e_hi")
        e_lo = sem("e_lo")
        y_hi = sem("y_hi")
        y_lo = sem("y_lo")
        fin_tr = sem("fin_tr")
        fin_cp = sem("fin_cp")
        chain = sem("chain")
        pchain = sem("pchain")
        dma_out = sem("dma_out")
        dma_mid = sem("dma_mid")

        START = [(bank, k // 2, 4 * (k % 2)) for k, bank in enumerate((6, 7, 0, 1))]
        START += [(bank, k // 2, 4 * (k % 2)) for k, bank in enumerate((2, 4, 5, 7, 0, 1))]
        MEM_STARTS, FIRST_STARTS = 4, 7

        block = ctx.enter_context(nc.Block())

        def wait_out(eng, l, tile):
            unit, last, mids = OUT_SIGNAL[tile]
            if last:
                eng.wait_ge(unit_done, UNIT_OF[layer_units(l)[unit]] + 1)
            else:
                eng.wait_ge(out_mm, l * OUT_MIDS + mids)

        def unit_source(u):
            kind, l, i = u
            if kind == "mk":
                return A["w_mem_k"][l].rearrange("(k p) n -> p k n", p=P)
            if kind == "mv":
                return A["w_mem_v"][l].rearrange("(k p) n -> p k n", p=P)
            if kind == "z":
                return A["w_in"][l].rearrange("(k p) n -> p k n", p=P)[:, :, Z_COLS[i]:Z_COLS[i] + 256]
            if kind == "pconv":
                return A["p_conv"][l].rearrange("(k p) n -> p k n", p=P)
            if kind == "pmem":
                return A["p_mem"][l].rearrange("(k p) n -> p k n", p=P)
            if kind == "wo":
                return A["w_o"][l].rearrange("(k p) n -> p k n", p=P)[:, :, 256 * i:256 * i + 256]
            if kind == "fg":
                return A["ffn_w_gate"][0].rearrange("(k p) n -> p k n", p=P)[:, :, 256 * i:256 * i + 256]
            if kind == "fu":
                return A["ffn_w_up"][0].rearrange("(k p) n -> p k n", p=P)[:, :, 256 * i:256 * i + 256]
            assert kind == "fd"
            return A["ffn_w_down"][0][256 * i:256 * i + 256, :].rearrange("(k p) n -> p k n", p=P)

        def tiled(buf, width):
            return buf[:, :].rearrange("p (k n) -> p k n", n=width)

        @block.sync
        def _(sp):
            for t in range(2):
                sp.dma_start(mstage[:, t, :], A["mem_prompt"][0, 128 * t:128 * t + 128, :]).then_inc(ld_mem, 16)
            for n, u in enumerate(STREAM):
                if n == 1:
                    for t in range(2):
                        sp.dma_start(xstage[:, t, :], A["x_prompt"][0, 128 * t:128 * t + 128, :]).then_inc(ld_x, 16)
                    sp.dma_start(xstage[0:64, 2, :], A["x_sample"].rearrange("b t d -> (b t) d")).then_inc(ld_x, 16)
                s = n % RING
                if n >= RING:
                    sp.wait_ge(unit_done, n - RING + 1)
                if u[0] == "pattn":
                    rows = A["p_attn"][u[1]].rearrange("(a g d) n -> a d g n", a=2, g=4)
                    for a in range(2):
                        sp.dma_start(tiled(raw[s], 512)[64 * a:64 * a + 64],
                                     rows[a, :, :, 512 * u[2]:512 * u[2] + 512]).then_inc(ld[s], 16)
                else:
                    src = unit_source(u)
                    sp.dma_start(tiled(raw[s], src.shape[2]), src).then_inc(ld[s], 16)

            def expert_unit(step, e, n):
                kind, i = EXPERT[n]
                s = n % RING_MOE
                sp.wait_ge(unit_done, step * NX + (N_DENSE - RING_MOE + n + 1))
                if kind == "d":
                    src = A["exp_w_down"][0][bass.ds(e, 1), 256 * i:256 * i + 256, :]
                    sp.dma_start(tiled(raw_moe[s], D), src.rearrange("o (k p) n -> p (o k) n", p=P)).then_inc(ld[s], 16)
                    return
                rows = slice(0, D // 2) if kind == "a" else slice(D // 2, D)
                for half, name in enumerate(("exp_w_gate", "exp_w_up")):
                    src = A[name][0][bass.ds(e, 1), rows, 256 * i:256 * i + 256]
                    sp.dma_start(tiled(raw_moe[s], 512)[:, :, 256 * half:256 * half + 256],
                                 src.rearrange("o (k p) n -> p (o k) n", p=P)).then_inc(ld[s], 16)

            sp.wait_ge(unit_done, N_DENSE)
            sp.wait_ge(dma_mid, 16 * (8 + 20 * 2))
            with sp.Fori(0, NE - 1) as step:
                for n in range(NX):
                    expert_unit(step, step, n)
            sp.wait_ge(rt_total, 1)
            total = sp.value_load(total_i[0:1, 0:1], min_val=NE, max_val=ROUNDS * NE)
            with sp.Fori(NE - 1, total) as step:
                for n in range(NX):
                    expert_unit(step, step % NE, n)
            for n in range(AHEAD):
                expert_unit(total, 0, n)

        @block.gpsimd
        def _(pool):
            steps = [0]

            def link(ins):
                steps[0] += 1
                ins.then_inc(pchain, 1)
                pool.wait_ge(pchain, steps[0])

            link(pool.memset(ident[:, :], 0.0))
            pool.affine_select(out=ident[:, :], in_=ident[:, :], compare_op=ALU.not_equal, fill=1.0,
                               base=0, pattern=[[-1, P]], channel_multiplier=1).then_inc(const, 1)
            pool.memset(mean_of[:, :], 1.0 / D).then_inc(const, 1)
            link(pool.memset(mask_win[:, :], 0.0))
            pool.affine_select(out=mask_win[:, 0:128], in_=mask_win[:, 0:128], compare_op=ALU.is_gt,
                               fill=NEG, base=0, pattern=[[1, P]], channel_multiplier=-1).then_inc(const, 1)
            pool.affine_select(out=mask_win[:, 128:256], in_=mask_win[:, 128:256], compare_op=ALU.is_ge,
                               fill=NEG, base=0, pattern=[[-1, P]], channel_multiplier=1).then_inc(const, 1)
            pool.memset(eps[:, :], EPS).then_inc(const, 1)
            pool.iota(row_i[:, 0:1], pattern=[[0, 1]], base=0, channel_multiplier=1).then_inc(const, 1)
            pool.iota(iota_i[:, :], pattern=[[1, P]], base=0, channel_multiplier=0).then_inc(const, 1)
            for i, name in enumerate(("ln1_g", "ln1_b", "ln2_g", "ln2_b")):
                pool.dma_start(vstage[16 * i:16 * i + 16, :],
                               A[name].rearrange("l (k p) -> (l k) p", p=P)).then_inc(ld_vec, 16)
            pool.dma_start(vstage[64:76, :], A["conv_w"].rearrange("l w (k p) -> (l w k) p", p=P)).then_inc(ld_vec, 16)

            def load_mem_k(l, g):
                pool.dma_start(kstage[:, :, :, :].rearrange("p b k n -> p (b k) n"),
                               A["cache_mem_k"][l, 4 * g:4 * g + 4].rearrange("b (k p) h d -> p (b k) (h d)", p=P)
                               ).then_inc(ld_memk, 16)

            def load_mem_v(l, g):
                pool.dma_start(mem_v[:, :, :, :].rearrange("p b k n -> p (b k) n"),
                               A["cache_mem_v"][l, 4 * g:4 * g + 4].rearrange("b (k p) h d -> p (b k) (h d)", p=P)
                               ).then_inc(ld_memv, 16)

            load_mem_k(0, 0)
            load_mem_v(0, 0)
            for l in range(2):
                pool.dma_start(sink_p[:, l, :], A["sink"][l:l + 1, :].to_broadcast([P, 8])).then_inc(ld_const, 16)
                for kv in range(2):
                    for b in range(4):
                        pool.dma_start(
                            sink_s[32 * b:32 * b + 32, l, kv:kv + 1],
                            A["sink"][l, 4 * kv:4 * kv + 4].unsqueeze(1).to_broadcast([4, 8]).unsqueeze(2)
                        ).then_inc(ld_const, 16)

            for l in range(2):
                for name, out in (("cache_win_k", "win_k_sample"), ("cache_win_v", "win_v_sample")):
                    pool.dma_start(O[out][l, :, 0:P - TS].rearrange("b j h d -> b (j h d)"),
                                   A[name][l, :, TS:P].rearrange("b j h d -> b (j h d)")).then_inc(dma_out, 16)

            for l in range(2):
                for i, (buf, name) in enumerate(((mtok, "mem_k_prompt"), (mv, "mem_v_prompt"))):
                    pool.wait_ge(mem_cp, 2 * l + i + 1)
                    for t in range(2):
                        pool.dma_start(O[name][l, 0, 128 * t:128 * t + 128].rearrange("m h d -> m (h d)"),
                                       buf[:, l, t, :]).then_inc(dma_mid, 16)

            for l in range(2):
                e0, j0 = l * N_EVENTS, l * NJ
                if l == 0:
                    pool.wait_ge(unit_done, 4)
                else:
                    pool.wait_ge(unit_done, UNIT_OF[("fd", 0, NBLK - 1)] + 1)
                pool.memset(qm_diag[:, :, :, :], 0.0).then_inc(zeroed, 1)
                pool.memset(uext[:, :, :], 0.0).then_inc(zeroed, 1)
                pool.dma_start(ustage[:, :], A["cache_conv"][l].rearrange("b r c -> (b r) c")).then_inc(ld_conv, 16)
                pool.wait_ge(tr_mm, e0 + EVENT_NO[("memk", 0, 1)] + 1)
                load_mem_k(l, 1)
                pool.wait_ge(tr_mm, e0 + EVENT_NO[("memk", 1, 1)] + 1)
                pool.dma_start(wstage[:, :, :], A["cache_win_k"][l].rearrange("b j h d -> j b (h d)")).then_inc(ld_wink, 16)
                pool.wait_ge(pv_mm, j0 + 3)
                load_mem_v(l, 1)
                pool.wait_ge(sc_mm, j0 + 4)
                pool.dma_start(win_v[:, :, :], A["cache_win_v"][l].rearrange("b j h d -> j b (h d)")).then_inc(ld_winv, 16)
                pool.wait_ge(tr_cp, e0 + EVENT_NO[("kvtok", 0, 0)] + 1)
                for i, kind in enumerate("kv"):
                    pool.dma_start(O[f"win_{kind}_prompt"][l, 0].rearrange("j h d -> j (h d)"),
                                   kvtok[:, i, 1, :]).then_inc(dma_mid, 16)
                    for b in range(NB):
                        pool.dma_start(O[f"win_{kind}_sample"][l, b, P - TS:P].rearrange("t h d -> t (h d)"),
                                       kvtok[TS * b:TS * b + TS, i, 2, :]).then_inc(dma_mid, 16)
                pool.wait_ge(tr_cp, e0 + EVENT_NO[("conv", 0, 0)] + 1)
                pool.dma_start(O["conv_prompt"][l, 0], uout[0:2, :]).then_inc(dma_mid, 16)
                pool.dma_start(O["conv_sample"][l].rearrange("b r c -> (b r) c"), uout[2:18, :]).then_inc(dma_mid, 16)
                if l == 0:
                    pool.wait_ge(tr_mm, e0 + EVENT_NO[("wink", 0, 0)] + 1)
                    load_mem_k(1, 0)
                    pool.wait_ge(pv_mm, j0 + 4)
                    load_mem_v(1, 0)
                pool.wait_ge(dma_mid, 16 * (8 + 20 * (l + 1)))
            pool.wait_ge(unit_done, N_DENSE)
            pool.dma_start(rw[:, :, :], A["router_w"][0].rearrange("(k p) e -> p k e", p=P)).then_inc(ld_const, 16)
            pool.dma_start(rb[:, :], A["router_b"][0:1, :].to_broadcast([P, NE])).then_inc(ld_const, 16)
            link(pool.memset(ones[:, :], 1.0))
            pool.affine_select(out=before[:, :], in_=ones[:, :], compare_op=ALU.is_gt, fill=0.0,
                               base=0, pattern=[[1, P]], channel_multiplier=-1).then_inc(const, 1)
            for t, (t0, tn) in enumerate(TILES):
                pool.wait_ge(fin_cp, 2 * t + 2)
                dst = (O["y_prompt"][0, t0:t0 + tn, :] if t < 2
                       else O["y_sample"].rearrange("b t d -> (b t) d"))
                pool.dma_start(dst, yout[0:tn, t, :]).then_inc(dma_out, 16)
            pool.wait_ge(dma_mid, 16 * (8 + 20 * 2))
            pool.wait_ge(dma_out, 16 * 7)
        CONSTS = 7
        CONST_LOADS = 18 * 16

        @block.scalar
        def _(act):
            def hi(n):
                if n >= N_DENSE:
                    return
                act.wait_ge(ld[n % RING], LD_VALUE[n])
                if n >= HI_RING:
                    act.wait_ge(unit_done, n - HI_RING + 1)
                act.activation(high[n % HI_RING][:, :], raw[n % RING][:, :], ACT.Copy).then_inc(hi_done, 1)

            def start_part(k):
                act.wait_ge(start_tr, k + 1)
                bank, t, f = START[k]
                t0, tn = TILES[t]
                src = ps[:, bank, :].rearrange("p (f t) -> p f t", t=P)[:, :, 0:tn]
                act.activation((mTh if k < MEM_STARTS else xh)[:, f:f + 4, t0:t0 + tn], src, ACT.Copy).then_inc(start_hi, 1)

            for k in range(MEM_STARTS):
                start_part(k)
            hi(0)
            for k in range(MEM_STARTS, FIRST_STARTS):
                start_part(k)
            hi(1)
            for n in range(4):
                hi(n + AHEAD)
                if n == 0:
                    for k in range(FIRST_STARTS, len(START)):
                        start_part(k)
                if n % 2 == 1:
                    l = n // 2
                    act.wait_ge(mkT_tr, l + 1)
                    act.activation(mkT[:, l, :, :], ps[:, 4 + l, :].rearrange("p (a m) -> p a m", m=256),
                                   ACT.Copy).then_inc(mkT_cp, 1)
            act.wait_ge(const, CONSTS)

            def event_copy(l, e):
                kind, g, r = e
                act.wait_ge(tr_mm, l * N_EVENTS + EVENT_NO[e] + 1)
                if kind == "memk":
                    act.activation(mem_kT[:, 2 * r:2 * r + 2, :, :],
                                   ps_tr[:, :, :].rearrange("p b (a m) -> p b a m", m=256), ACT.Copy).then_inc(tr_cp, 1)
                elif kind == "kvtok":
                    for i in range(2):
                        act.activation(kvtok[:, i, 0:2, :], ps_tr[:, i, 0:256].rearrange("p (t c) -> p t c", c=P), ACT.Copy)
                        act.activation(kvtok[0:64, i, 2, :], ps_tr[0:64, i, 256:384], ACT.Copy)
                    act.wait_ge(zeroed, 2 * l + 2)
                    act.activation(uext[:, :, NP + 2:].rearrange("p f (b t) -> p f b t", t=TS + 2)[:, :, :, 0:2],
                                   ps_tr[:, 0, 384:416].rearrange("p (f b r) -> p f b r", f=2, r=2),
                                   ACT.Copy).then_inc(tr_cp, 1)
                elif kind == "conv":
                    act.activation(uout[:, :], ps_tr[0:18, 0, 0:256], ACT.Copy).then_inc(tr_cp, 1)
                elif kind == "wink":
                    act.activation(win_kT[:, :, :], ps_tr[:, :, :].rearrange("p b (s m) -> p (b s) m", m=P),
                                   ACT.Copy).then_inc(tr_cp, 1)
                else:
                    if l * NJ + g >= 1:
                        act.wait_ge(pv_mm, l * NJ + g)
                    jk, ji = JOBS[g]
                    if jk == "smem":
                        act.activation(pT[:, :, 0:128], ps_tr[:, :, 0:128], ACT.Copy).then_inc(tr_cp, 1)
                    elif jk == "pmem" or (jk == "pwin" and ji[0] == 1):
                        act.activation(pT[:, :, :], ps_tr[:, :, :], ACT.Copy).then_inc(tr_cp, 1)
                    elif jk == "pwin":
                        act.activation(pT[:, 0, :], ps_tr[:, 0, :], ACT.Copy).then_inc(tr_cp, 1)
                    else:
                        act.activation(pT[:, 0, :], ps_tr[:, 0, :], ACT.Copy)
                        act.activation(pT[0:64, 1, :], ps_tr[0:64, 1, :], ACT.Copy).then_inc(tr_cp, 1)

            def exps(l, j):
                kind, idx = JOBS[j]
                n, w = job_shape(kind, idx)
                win = kind in ("pwin", "swin")
                act.wait_ge(sc_cp, l * NJ + j + 1)
                if not win and l * NJ + j >= 1:
                    e = ("probs", (j - 1) % NJ, 0)
                    act.wait_ge(tr_mm, (l if j else l - 1) * N_EVENTS + EVENT_NO[e] + 1)
                if l == 0 and j == 0:
                    act.wait_ge(dma_mid, 8 * 16)
                for g in range(n):
                    src, scale = (sc, 1.0) if win else (ps_sc, SCALE)
                    last = act.activation(sc[:, g, 0:w], src[:, g, 0:w], ACT.Exp, bias=small[:, 8 + g:9 + g],
                                          scale=scale, accum_out=small[:, 16 + g:17 + g])
                if win:
                    last = act.activation(small[:, 24:28], small[:, 12:16], ACT.Exp)
                last.then_inc(exp_done, 1)

            def attention_out(l, j, eng_hi):
                kind, idx = JOBS[j]
                if kind == "pmem":
                    return [("om", slice(0, 128), lambda b: b[:, 0:2, 128 * idx:128 * idx + 128],
                             ps[:, 3, 0:256].rearrange("p (a t) -> p a t", t=128))]
                if kind == "smem":
                    out = []
                    for a in range(2):
                        for p in range(2):
                            h = slice(64 * a, 64 * a + 64)
                            src = ps[h, 3, 128 * p:128 * p + 128].rearrange("p (b c) -> p b c", c=32)[
                                :, :, (2 * p + a) * 8:(2 * p + a) * 8 + 8]
                            out.append(("om", h, lambda b, h=h, p=p: b[h, p, NP + 32 * idx:NP + 32 * idx + 32]
                                        .rearrange("p (b t) -> p b t", t=8), src))
                    return out
                if kind == "pwin":
                    n, kv = idx
                    h = slice(64 * kv, 64 * kv + 64)
                    return [("oa", h, lambda b: b[h, :, 128 * n:128 * n + 128],
                             ps[h, 3, :].rearrange("p (g t) -> p g t", t=128))]
                out = []
                for kv in range(2):
                    h = slice(64 * kv, 64 * kv + 64)
                    out.append(("oa", h, lambda b, h=h: b[h, :, NP:T].rearrange("p g (b t) -> p g b t", t=8),
                                ps[h, 3, 256 * kv:256 * kv + 256].rearrange("p (b g t) -> p g b t", g=4, t=8)))
                return out

            def o_copy(l, j):
                act.wait_ge(pv_mm, l * NJ + j + 1)
                for which, _, dst, src in attention_out(l, j, True):
                    last = act.activation(dst(oah if which == "oa" else omh), src, ACT.Copy)
                last.then_inc(o_hi, 1)

            def z_copy(l, f):
                n = l * len(OUTS) + OUT_NO[("z", f)]
                wait_out(act, l, ("z", f))
                src = ps[:, n % 3, 0:T]
                if 2 <= f < 6:
                    for a in range(2):
                        head = 2 * (f - 2) + a
                        kv, g = head // 4, head % 4
                        to, of = slice(64 * kv, 64 * kv + 64), slice(64 * a, 64 * a + 64)
                        act.activation(qT[to, g, :], src[of, 0:NP], ACT.Copy)
                        last = act.activation(qS[to, :, g, :], src[of, NP:T].rearrange("p (b t) -> p b t", t=TS), ACT.Copy)
                elif 6 <= f < 8:
                    last = act.activation(kvT[:, f - 6, :], src, ACT.Copy)
                elif 8 <= f < 14:
                    last = act.activation(hbc[:, f - 8, :], src, ACT.Copy)
                elif f < 2:
                    p = f
                    act.wait_ge(zeroed, 2 * l + 2)
                    act.activation(qmT[:, p, :], src[:, 0:NP], ACT.Copy)
                    for a in range(2):
                        h = slice(64 * a, 64 * a + 64)
                        last = act.activation(qm_diag[h, p, :, (2 * p + a) * 8:(2 * p + a) * 8 + 8],
                                              src[h, NP:T].rearrange("p (b t) -> p b t", t=8), ACT.Copy)
                else:
                    g = (f - 14) % 8
                    if f >= 22:
                        act.wait_ge(merge_done, l * len(MERGES)
                                    + MERGE_NO[("pconv" if f < 30 else "pmem", g)] + 1)
                    last = act.activation(gate[:, g, :], src, ACT.Tanh, scale=0.5)
                last.then_inc(z_cp, 1)

            def layer_norm(L, split, vec):
                sq = sq_last if L == 3 else sq_dense
                if L in (0, 2):
                    act.wait_ge(dma_mid, 16 * (8 + 20 * (L // 2 + 1)))
                act.activation(row_f[:, 2:3], eps[:, 0:1], ACT.Sqrt)
                for f in range(KD):
                    act.wait_ge(centered, KD * L + f + 1)
                    act.activation(sq[:, f, :], x[:, f, :], ACT.Square).then_inc(squared, 1)
                act.wait_ge(var_mm, KD * L + KD)
                act.activation(std[:, :], ps[:, VAR, 0:T], ACT.Sqrt, bias=eps[:, 0:1]).then_inc(std_done, 1)
                for f in range(KD):
                    act.wait_ge(normed, KD * L + f + 1)
                    g, b = vecs[:, vec + f:vec + f + 1], vecs[:, vec + 16 + f:vec + 17 + f]
                    if split:
                        act.activation(xh[:, f, :], x[:, f, :], ACT.Identity, scale=g, bias=b).then_inc(xh_done, 1)
                    act.activation(x[:, f, :], x[:, f, :], ACT.Identity, scale=g, bias=b).then_inc(x_done, 1)

            def mixer(l):
                units = layer_units(l)
                for i, u in enumerate(units):
                    n = UNIT_OF[u]
                    hi(n + AHEAD)
                    if u[0] == "z":
                        z_copy(l, 2 * u[2])
                        z_copy(l, 2 * u[2] + 1)
                        if u[2] == 7:
                            act.wait_ge(conv_done, l + 1)
                            act.activation(och[:, :, :], hbc[:, 4:6, :], ACT.Copy).then_inc(och_done, 1)
                    for work in SLOTS.get(i, ()):
                        if work[0] == "pv":
                            o_copy(l, work[1])
                        elif work[0] == "event":
                            event_copy(l, work[1:])
                        else:
                            exps(l, work[1])
                    if u[0] == "pattn":
                        for f in range(4 * u[2], 4 * u[2] + 4):
                            act.wait_ge(merge_done, l * len(MERGES) + MERGE_NO[("pattn", f)] + 1)
                            act.activation(xh[:, f, :], merged[:, f, :], ACT.Copy, scale=0.5).then_inc(mh_done, 1)

            mixer(0)
            layer_norm(0, True, 0)
            for i in range(NBLK):
                for half in range(2):
                    hi(UNIT_OF[("fg" if half == 0 else "fu", 0, i)] + AHEAD)
                    if half == 0 and i >= 1:
                        act.wait_ge(ff_h, i)
                        act.activation(hTh[:, 2 * i - 2:2 * i, :], hfull[:, (i - 1) % 2, :, :], ACT.Copy).then_inc(ff_hi, 1)
                    if half == 1:
                        act.wait_ge(unit_done, UNIT_OF[("fg", 0, i)] + 1)
                        if i >= 2:
                            act.wait_ge(ff_h, i - 1)
                        act.activation(silu[:, i % 2, :, :], ps[:, 4 * (i % 2):4 * (i % 2) + 2, 0:T], ACT.Silu).then_inc(ff_silu, 1)
            act.wait_ge(ff_h, NBLK)
            act.activation(hTh[:, 2 * NBLK - 2:2 * NBLK, :], hfull[:, (NBLK - 1) % 2, :, :], ACT.Copy).then_inc(ff_hi, 1)
            for i in range(NBLK):
                hi(UNIT_OF[("fd", 0, i)] + AHEAD)
            layer_norm(1, True, 32)
            mixer(1)
            layer_norm(2, False, 8)

            def hi_moe(step, n):
                s = n % RING_MOE
                loads = LDX_VALUE[n] if n < NX else LDX_STEP[s] + LDX_VALUE[n - NX]
                act.wait_ge(ld[s], step * LDX_STEP[s] + (LD_BASE[s] + loads))
                act.wait_ge(unit_done, step * NX + (N_DENSE + n - HI_RING + 1))
                act.activation(high[(N_DENSE + n) % HI_RING][:, :], raw_moe[s][:, :], ACT.Copy).then_inc(hi_done, 1)

            for k in range(6):
                t0, tn = TILES[k // 2]
                act.wait_ge(xt_mm, k + 1)
                act.activation(xtokh[0:tn, k // 2, 512 * (k % 2):512 * (k % 2) + 512], ps[0:tn, 2 + k, :],
                               ACT.Copy).then_inc(xt_hi, 1)
            for t in range(3):
                act.wait_ge(rt_top, t + 1)
                tn = TILES[t][1]
                act.activation(pair[0:tn, t, 1:2], pair[0:tn, t, 0:1], ACT.Exp).then_inc(rt_exp, 1)
            for n in range(AHEAD):
                hi_moe(0, n)

            def gathered_hi(first, c):
                act.wait_ge(side_mm, first + (c + 1))
                act.activation(xnh[:, 2 * c:2 * c + 2, :], ps[:, 6 + c % 2, 0:256].rearrange("p (f s) -> p f s", s=P),
                               ACT.Copy).then_inc(xe_hi, 1)

            def hidden_hi(step, i):
                act.wait_ge(e_tr, step * NBLK + (i + 1))
                act.activation(heh[:, i % 2, :, :], ps[:, 4 + i % 2, 0:256].rearrange("p (f s) -> p f s", s=P),
                               ACT.Copy).then_inc(e_hi, 1)

            for c in range(4):
                gathered_hi(0, c)
            act.wait_ge(xe_hi, 4)
            act.activation(xeh[:, :, :], xnh[:, :, :].bitcast(F32), ACT.Copy).then_inc(xe_ok, 1)
            act.wait_ge(rt_total, 1)
            total = act.value_load(total_i[0:1, 0:1], min_val=NE, max_val=ROUNDS * NE)
            with act.Fori(0, total) as step:
                for n, (kind, i) in enumerate(EXPERT):
                    if (kind, i) == ("d", NBLK - 2):
                        hidden_hi(step, NBLK - 1)
                        act.wait_ge(unit_done, step * NX + (N_DENSE + n))
                        act.wait_ge(xe_hi, step * 4 + 8)
                        act.activation(xeh[:, :, :], xnh[:, :, :].bitcast(F32), ACT.Copy).then_inc(xe_ok, 1)
                    hi_moe(step, n + AHEAD)
                    if kind == "a" and i >= 1:
                        hidden_hi(step, i - 1)
                    if kind == "b":
                        act.wait_ge(unit_done, step * NX + (N_DENSE + n + 1))
                        act.activation(sil[:, i % 2, :], ps[:, 2 + i % 2, 0:256], ACT.Silu).then_inc(e_silu, 1)
                    if n in SIDE and SIDE[n][0] == "gather":
                        gathered_hi(step * 14 + 14, SIDE[n][1])
                    if kind == "d" and i == NBLK - 1:
                        act.wait_ge(unit_done, step * NX + (N_DENSE + NX))
                        act.wait_ge(slot_ok, step + 2)
                        act.activation(ygh[:, :], ps[:, 0:2, :].rearrange("p b n -> p (b n)"), ACT.Copy,
                                       scale=gs_cur[:, 0:1]).then_inc(y_hi, 1)
            layer_norm(3, False, 40)

        @block.vector
        def _(dve):
            links = [0]

            def link(ins):
                links[0] += 1
                ins.then_inc(chain, 1)
                dve.wait_ge(chain, links[0])

            def lo(n):
                if n >= N_DENSE:
                    return
                dve.wait_ge(hi_done, n + 1)
                dve.tensor_tensor(low[n % RING][:, :], raw[n % RING][:, :],
                                  high[n % HI_RING][:, :].bitcast(F32), ALU.subtract).then_inc(lo_done, 1)

            def start_part(k):
                bank, t, f = START[k]
                t0, tn = TILES[t]
                src = ps[:, bank, :].rearrange("p (f t) -> p f t", t=P)[:, :, 0:tn]
                high_part, low_part = (mTh, mTl) if k < MEM_STARTS else (xh, xl)
                dve.wait_ge(start_hi, k + 1)
                if k >= MEM_STARTS:
                    dve.tensor_copy(x[:, f:f + 4, t0:t0 + tn], src)
                dve.tensor_tensor(low_part[:, f:f + 4, t0:t0 + tn], src,
                                  high_part[:, f:f + 4, t0:t0 + tn].bitcast(F32), ALU.subtract).then_inc(start_lo, 1)

            for k in range(MEM_STARTS):
                start_part(k)
            lo(0)
            for k in range(MEM_STARTS, FIRST_STARTS):
                start_part(k)
            lo(1)
            for n in range(4):
                lo(n + AHEAD)
                l, is_v = n // 2, n % 2
                dve.wait_ge(unit_done, n + 1)
                dve.tensor_copy((mv if is_v else mtok)[:, l, :, :],
                                ps[:, 3 if n % 2 == 0 else 6, :].rearrange("p (t c) -> p t c", c=256)).then_inc(mem_cp, 1)
                if n == 0:
                    for k in range(FIRST_STARTS, len(START)):
                        start_part(k)
                if n == 3:
                    dve.wait_ge(start_tr, len(START) + 1)
                    dve.tensor_copy(vecs[:, :], ps[:, 2, 0:76]).then_inc(vconst, 1)
            dve.wait_ge(const, CONSTS)
            link(dve.tensor_scalar(row_i[:, 1:2], row_i[:, 0:1], 7, None, ALU.bitwise_and))
            link(dve.tensor_scalar(row_i[:, 2:3], row_i[:, 0:1], 5, None, ALU.logical_shift_right))
            link(dve.tensor_copy(row_f[:, 0:2], row_i[:, 1:3]))
            link(dve.tensor_copy(iota_f[:, :], iota_i[:, :]))
            for bg in range(2):
                first, last_key = row_f[:, 2:3], row_f[:, 3:4]
                link(dve.tensor_scalar(mask_dec[:, bg, 0:128], iota_f[:, :], row_f[:, 0:1], NEG, ALU.is_le, ALU.mult))
                link(dve.tensor_scalar(first, row_f[:, 1:2], 8.0, 32.0 * bg, ALU.mult, ALU.add))
                link(dve.tensor_tensor(last_key, first, row_f[:, 0:1], ALU.add))
                link(dve.tensor_scalar(mask_dec[:, bg, 128:192], iota_f[:, 0:64], first, NEG, ALU.is_lt, ALU.mult))
                link(dve.tensor_scalar(small[:, 0:64], iota_f[:, 0:64], last_key, NEG, ALU.is_gt, ALU.mult))
                link(dve.tensor_tensor(mask_dec[:, bg, 128:192], mask_dec[:, bg, 128:192], small[:, 0:64], ALU.add))
            def scores(l, j):
                kind, idx = JOBS[j]
                n, w = job_shape(kind, idx)
                dve.wait_ge(sc_mm, l * NJ + j + 1)
                if kind in ("smem", "pmem"):
                    if l * NJ + j >= 1:
                        dve.wait_ge(exp_done, l * NJ + j)
                    link(dve.tensor_reduce(small[:, 0:n], ps_sc[:, 0:n, 0:w], AX, ALU.max))
                    dve.tensor_scalar(small[:, 8:8 + n], small[:, 0:n], -SCALE, None, ALU.mult).then_inc(sc_cp, 1)
                    return
                if l * NJ + j >= 1:
                    e = ("probs", (j - 1) % NJ, 0)
                    dve.wait_ge(tr_mm, (l if j else l - 1) * N_EVENTS + EVENT_NO[e] + 1)
                nmax, shift = small[:, 8:8 + n], small[:, 12:12 + n]
                if l == 0 and JOBS[j] == ("pwin", (0, 0)):
                    dve.wait_ge(ld_const, CONST_LOADS)
                    link(dve.tensor_scalar(sink_p[:, :, :], sink_p[:, :, :], -1.0, None, ALU.mult))
                    link(dve.tensor_scalar(sink_s[:, :, :], sink_s[:, :, :], -1.0, None, ALU.mult))
                if kind == "pwin":
                    mask = mask_win[:, 256 - w:256].unsqueeze(1).to_broadcast([P, n, w])
                    nsink = sink_p[:, l, 4 * idx[1]:4 * idx[1] + 4]
                    link(dve.scalar_tensor_tensor(sc[:, 0:n, 0:w], ps_sc[:, 0:n, 0:w], SCALE, mask, ALU.mult, ALU.add))
                else:
                    nsink = sink_s[:, l, :].unsqueeze(2).to_broadcast([P, 2, 2])
                    for kv in range(2):
                        link(dve.scalar_tensor_tensor(sc[:, 2 * kv:2 * kv + 2, 0:w], ps_sc[:, 2 * kv:2 * kv + 2, 0:w],
                                                      SCALE, mask_dec[:, :, :], ALU.mult, ALU.add))
                link(dve.tensor_reduce(small[:, 0:n], sc[:, 0:n, 0:w], AX, ALU.max))
                link(dve.tensor_scalar(small[:, 4:4 + n], small[:, 0:n], -1.0, None, ALU.mult))
                if kind == "swin":
                    v = lambda c: small[:, c:c + 4].rearrange("p (a b) -> p a b", b=2)
                    link(dve.tensor_tensor(v(8), v(4), nsink, ALU.min))
                    dve.tensor_tensor(v(12), v(8), nsink, ALU.subtract).then_inc(sc_cp, 1)
                else:
                    link(dve.tensor_tensor(nmax, small[:, 4:8], nsink, ALU.min))
                    dve.tensor_tensor(shift, nmax, nsink, ALU.subtract).then_inc(sc_cp, 1)

            def normalise(l, j):
                kind, idx = JOBS[j]
                n, w = job_shape(kind, idx)
                dve.wait_ge(exp_done, l * NJ + j + 1)
                den = small[:, 16:16 + n]
                if kind in ("pwin", "swin"):
                    link(dve.tensor_tensor(den, den, small[:, 24:28], ALU.add))
                link(dve.reciprocal(small[:, 20:20 + n], den))
                dve.tensor_tensor(sc[:, 0:n, 0:w], sc[:, 0:n, 0:w],
                                  small[:, 20:20 + n].unsqueeze(2).to_broadcast([P, n, w]), ALU.mult).then_inc(probs, 1)

            def o_low(l, j):
                dve.wait_ge(o_hi, l * NJ + j + 1)
                kind, idx = JOBS[j]
                if kind == "pmem":
                    parts = [(omh, oml, slice(0, 128), lambda b: b[:, 0:2, 128 * idx:128 * idx + 128],
                              ps[:, 3, 0:256].rearrange("p (a t) -> p a t", t=128))]
                elif kind == "smem":
                    parts = []
                    for a in range(2):
                        for p in range(2):
                            h = slice(64 * a, 64 * a + 64)
                            src = ps[h, 3, 128 * p:128 * p + 128].rearrange("p (b c) -> p b c", c=32)[
                                :, :, (2 * p + a) * 8:(2 * p + a) * 8 + 8]
                            parts.append((omh, oml, h, lambda b, h=h, p=p: b[h, p, NP + 32 * idx:NP + 32 * idx + 32]
                                          .rearrange("p (b t) -> p b t", t=8), src))
                elif kind == "pwin":
                    n, kv = idx
                    h = slice(64 * kv, 64 * kv + 64)
                    parts = [(oah, oal, h, lambda b: b[h, :, 128 * n:128 * n + 128],
                              ps[h, 3, :].rearrange("p (g t) -> p g t", t=128))]
                else:
                    parts = []
                    for kv in range(2):
                        h = slice(64 * kv, 64 * kv + 64)
                        parts.append((oah, oal, h, lambda b, h=h: b[h, :, NP:T].rearrange("p g (b t) -> p g b t", t=8),
                                      ps[h, 3, 256 * kv:256 * kv + 256].rearrange("p (b g t) -> p g b t", g=4, t=8)))
                for bh, bl, _, view, src in parts:
                    last = dve.tensor_tensor(view(bl), src, view(bh).bitcast(F32), ALU.subtract)
                last.then_inc(o_lo, 1)

            def conv(l):
                dve.wait_ge(z_cp, l * 38 + 14)
                dve.wait_ge(tr_cp, l * N_EVENTS + EVENT_NO[("kvtok", 0, 0)] + 1)
                dve.wait_ge(const, CONSTS)
                h, b_gate, c_gate = hbc[:, 0:2, :], hbc[:, 2:4, :], hbc[:, 4:6, :]
                smp = lambda s: uext[:, :, NP + 2:].rearrange("p f (b t) -> p f b t", t=TS + 2)[:, :, :, s:s + TS]
                bt = lambda a: a[:, :, NP:T].rearrange("p f (b t) -> p f b t", t=TS)
                link(dve.tensor_tensor(uext[:, :, 2:NP + 2], c_gate[:, :, 0:NP], h[:, :, 0:NP], ALU.mult))
                for f in range(2):
                    link(dve.tensor_tensor(smp(2)[:, f], bt(c_gate)[:, f], bt(h)[:, f], ALU.mult))
                for f in range(2):
                    w = lambda j: vecs[:, 64 + 6 * l + 2 * j + f:65 + 6 * l + 2 * j + f]
                    for out, u in ((c_gate[:, f, 0:NP], lambda s: uext[:, f, s:s + NP]),
                                   (bt(c_gate)[:, f], lambda s: smp(s)[:, f])):
                        link(dve.tensor_scalar(out, u(0), w(0), None, ALU.mult))
                        link(dve.scalar_tensor_tensor(out, u(1), w(1), out, ALU.mult, ALU.add))
                        link(dve.scalar_tensor_tensor(out, u(2), w(2), out, ALU.mult, ALU.add))
                dve.tensor_tensor(c_gate[:, :, :], c_gate[:, :, :], b_gate, ALU.mult).then_inc(conv_done, 1)

            def last_rows(l):
                dve.tensor_copy(ulast[:, :, 0:2], uext[:, :, NP:NP + 2])
                dve.tensor_copy(ulast[:, :, 2:18].rearrange("p f (b r) -> p f b r", r=2),
                                uext[:, :, NP + 2:].rearrange("p f (b t) -> p f b t", t=TS + 2)[:, :, :, TS:TS + 2]
                                ).then_inc(ulast_done, 1)

            def merge(l, kind, f):
                n = l * len(OUTS) + OUT_NO[(kind, f)]
                wait_out(dve, l, (kind, f))
                if kind == "pconv":
                    dve.scalar_tensor_tensor(merged[:, f, :], gate[:, f, :], 1.0, ps[:, n % 3, 0:T],
                                             ALU.add, ALU.mult).then_inc(merge_done, 1)
                else:
                    link(dve.scalar_tensor_tensor(gate[:, f, :], gate[:, f, :], 1.0, ps[:, n % 3, 0:T], ALU.add, ALU.mult))
                    dve.tensor_tensor(merged[:, f, :], merged[:, f, :], gate[:, f, :], ALU.add).then_inc(merge_done, 1)

            def residual(l, f):
                n = l * len(OUTS) + OUT_NO[("wo", f)]
                wait_out(dve, l, ("wo", f))
                dve.scalar_tensor_tensor(x[:, f, :], x[:, f, :], ALPHA, ps[:, n % 3, 0:T],
                                         ALU.mult, ALU.add).then_inc(resid, 1)

            def layer_norm(L, split):
                dve.wait_ge(mean_mm, L + 1)
                for f in range(KD):
                    dve.tensor_tensor(x[:, f, :], x[:, f, :], ps[:, MEAN, 0:T], ALU.subtract).then_inc(centered, 1)
                dve.wait_ge(std_done, L + 1)
                dve.reciprocal(std[:, :], std[:, :]).then_inc(rstd_done, 1)
                dve.wait_ge(rstd_done, L + 1)
                for f in range(KD + 2):
                    if f < KD:
                        dve.tensor_tensor(x[:, f, :], x[:, f, :], std[:, :], ALU.mult).then_inc(normed, 1)
                    if split and f >= 2:
                        dve.wait_ge(x_done, KD * L + f - 1)
                        dve.tensor_tensor(xl[:, f - 2, :], x[:, f - 2, :], xh[:, f - 2, :].bitcast(F32),
                                          ALU.subtract).then_inc(xl_done, 1)

            def mixer(l):
                pending = None
                for i, u in enumerate(layer_units(l)):
                    merging = u[0] in ("pconv", "pmem")
                    if merging:
                        for f in range(KD // 2):
                            merge(l, u[0], f)
                    lo(UNIT_OF[u] + AHEAD)
                    if u == ("z", l, 6):
                        conv(l)
                    if u == ("z", l, 8):
                        dve.wait_ge(och_done, l + 1)
                        dve.tensor_tensor(ocl[:, :, :], hbc[:, 4:6, :], och[:, :, :].bitcast(F32), ALU.subtract).then_inc(ocl_done, 1)
                        dve.wait_ge(ocl_done, l + 1)
                    if u == ("z", l, 6):
                        last_rows(l)
                    if merging:
                        for f in range(KD // 2, KD):
                            merge(l, u[0], f)
                    if pending is not None:
                        normalise(l, pending)
                        pending = None
                    for work in SLOTS.get(i, ()):
                        if work[0] == "pv":
                            o_low(l, work[1])
                        elif work[0] == "scores":
                            scores(l, work[1])
                            pending = work[1]
                    if u[0] == "pattn":
                        for f in range(4 * u[2], 4 * u[2] + 4):
                            merge(l, "pattn", f)
                            dve.wait_ge(mh_done, KD * l + f + 1)
                            dve.scalar_tensor_tensor(xl[:, f, :], merged[:, f, :], 0.5, xh[:, f, :].bitcast(F32),
                                                     ALU.mult, ALU.subtract).then_inc(ml_done, 1)
                    if u[0] == "wo":
                        residual(l, 2 * u[2])
                        residual(l, 2 * u[2] + 1)

            mixer(0)
            layer_norm(0, True)

            def ffn_low(i):
                dve.wait_ge(ff_hi, i + 1)
                dve.tensor_tensor(hTl[:, 2 * i:2 * i + 2, :], hfull[:, i % 2, :, :],
                                  hTh[:, 2 * i:2 * i + 2, :].bitcast(F32), ALU.subtract).then_inc(ff_lo, 1)

            for i in range(NBLK):
                lo(UNIT_OF[("fg", 0, i)] + AHEAD)
                if i >= 1:
                    ffn_low(i - 1)
                lo(UNIT_OF[("fu", 0, i)] + AHEAD)
                dve.wait_ge(ff_silu, i + 1)
                dve.wait_ge(unit_done, UNIT_OF[("fu", 0, i)] + 1)
                if i >= 2:
                    dve.wait_ge(ff_lo, i - 1)
                dve.tensor_tensor(hfull[:, i % 2, :, :], silu[:, i % 2, :, :],
                                  ps[:, 4 * (i % 2) + 2:4 * (i % 2) + 4, 0:T], ALU.mult).then_inc(ff_h, 1)
            ffn_low(NBLK - 1)
            for i in range(NBLK):
                lo(UNIT_OF[("fd", 0, i)] + AHEAD)
            for k, f in enumerate((4, 5, 6, 7, 0, 1, 2, 3)):
                if k < KD - 1:
                    dve.wait_ge(down_mm, k + 1)
                else:
                    dve.wait_ge(unit_done, UNIT_OF[("fd", 0, NBLK - 1)] + 1)
                dve.scalar_tensor_tensor(x[:, f, :], x[:, f, :], ALPHA, ps[:, f, 0:T], ALU.mult, ALU.add).then_inc(resid, 1)
            layer_norm(1, True)
            mixer(1)
            layer_norm(2, False)

            dve.wait_ge(x_done, KD * 3)
            dve.memset(pos[:, :, :], 1.0e6)
            dve.memset(gates[:, :, :], 0.0)
            dve.memset(slot_cur[:, :].bitcast(F32), 0.0).then_inc(slot_ok, 1)
            link(dve.memset(ygh[:, :].bitcast(F32), 0.0))
            dve.memset(ygl[:, :].bitcast(F32), 0.0).then_inc(y_lo, 1)
            for k in range(6):
                t0, tn = TILES[k // 2]
                dve.wait_ge(xt_hi, k + 1)
                cols = slice(512 * (k % 2), 512 * (k % 2) + 512)
                dve.tensor_tensor(xtokl[0:tn, k // 2, cols], ps[0:tn, 2 + k, :],
                                  xtokh[0:tn, k // 2, cols].bitcast(F32), ALU.subtract).then_inc(xt_lo, 1)
            dve.wait_ge(ld_const, CONST_LOADS + 32)
            dve.wait_ge(rt_mm, 1)
            for t, (t0, tn) in enumerate(TILES):
                r = slice(0, tn)
                link(dve.tensor_tensor(logit[r, t, :], ps[r, 0, 8 * t:8 * t + 8], rb[r, :], ALU.add))
                link(dve.max(top[r, t, :], logit[r, t, :]))
                link(dve.max_index(topi[r, t, :], top[r, t, :], logit[r, t, :]))
                dve.tensor_tensor(pair[r, t, 0:1], top[r, t, 1:2], top[r, t, 0:1], ALU.subtract).then_inc(rt_top, 1)
                link(dve.tensor_copy(topf[r, t, :], topi[r, t, :]))
                link(dve.tensor_scalar(oh1[r, t, :], iota_f[r, 0:8], topf[r, t, 0:1], None, ALU.is_equal))
                link(dve.tensor_scalar(oh2[r, t, :], iota_f[r, 0:8], topf[r, t, 1:2], None, ALU.is_equal))
                dve.tensor_tensor(chosen[r, t, :], oh1[r, t, :], oh2[r, t, :], ALU.add).then_inc(rt_sel, 1)
            for t, (t0, tn) in enumerate(TILES):
                r = slice(0, tn)
                dve.wait_ge(rt_exp, t + 1)
                link(dve.tensor_scalar(pair[r, t, 2:3], pair[r, t, 1:2], 1.0, None, ALU.add))
                link(dve.reciprocal(pair[r, t, 2:3], pair[r, t, 2:3]))
                link(dve.tensor_tensor(pair[r, t, 3:4], pair[r, t, 1:2], pair[r, t, 2:3], ALU.mult))
                link(dve.tensor_scalar(oh1[r, t, :], oh1[r, t, :], pair[r, t, 2:3], None, ALU.mult))
                link(dve.tensor_scalar(oh2[r, t, :], oh2[r, t, :], pair[r, t, 3:4], None, ALU.mult))
                for k in range(ROUNDS):
                    link(dve.tensor_tensor(gates[r, t, NE * k:NE * k + NE], oh1[r, t, :], oh2[r, t, :], ALU.add))
            dve.wait_ge(rt_rank, 1)
            for t, (t0, tn) in enumerate(TILES):
                r = slice(0, tn)
                link(dve.scalar_tensor_tensor(posm[r, t, :], chosen[r, t, :], -65536.0, ps[r, 1, 8 * t:8 * t + 8],
                                              ALU.mult, ALU.add))
                for k in range(ROUNDS):
                    link(dve.tensor_scalar(pos[r, t, NE * k:NE * k + NE], posm[r, t, :], 65536.0 - 128.0 * k, None, ALU.add))
            link(dve.tensor_reduce(cnt[:, 0:1], ps[:, 1, 24:32], AX, ALU.max))
            link(dve.tensor_scalar(cnt[:, 1:2], cnt[:, 0:1], 128.0, float(NE), ALU.is_gt, ALU.mult))
            link(dve.tensor_scalar(cnt[:, 2:3], cnt[:, 0:1], 256.0, float(NE), ALU.is_gt, ALU.mult))
            link(dve.tensor_tensor(cnt[:, 3:4], cnt[:, 1:2], cnt[:, 2:3], ALU.add))
            link(dve.tensor_scalar(cnt[:, 3:4], cnt[:, 3:4], float(NE), None, ALU.add))
            dve.tensor_copy(total_i[:, :], cnt[:, 3:4]).then_inc(rt_total, 1)
            link(dve.tensor_scalar(x[:, :, :], x[:, :, :], ALPHA, None, ALU.mult))

            def lo_moe(step, n):
                dve.wait_ge(hi_done, step * NX + (N_DENSE + n + 1))
                s = n % RING_MOE
                dve.tensor_tensor(low_moe[s][:, :], raw_moe[s][:, :],
                                  high[(N_DENSE + n) % HI_RING][:, :].bitcast(F32), ALU.subtract).then_inc(lo_done, 1)

            def one_hot(step):
                for t, (t0, tn) in enumerate(TILES):
                    dve.tensor_scalar(onehot[0:tn, t, :], iota_f[0:tn, :], pos[0:tn, t, bass.ds(step, 1)], None, ALU.is_equal)
                dve.tensor_copy(gcol[:, :].unsqueeze(2), gates[:, :, bass.ds(step, 1)]).then_inc(oh_done, 1)

            def gathered_lo(hi_before, c):
                dve.wait_ge(xe_hi, hi_before + (c + 1))
                dve.tensor_copy(xnl[:, 2 * c:2 * c + 2, :], ps[:, 6 + c % 2, 256:512].rearrange("p (f s) -> p f s", s=P)
                                ).then_inc(side_cp, 1)

            def slots_copy(first):
                dve.wait_ge(side_mm, first + 5)
                dve.tensor_copy(slot_next[:, :], ps[:, 6, 0:T]).then_inc(side_cp, 1)
                dve.wait_ge(side_mm, first + 6)
                dve.tensor_copy(gs_next[:, :], ps[:, 7, 0:1]).then_inc(side_cp, 1)

            def add_back(first, tiles):
                for f in tiles:
                    dve.wait_ge(side_mm, first + (f + 1))
                    dve.tensor_tensor(x[:, f, :], x[:, f, :], ps[:, 6 + f % 2, 0:T], ALU.add).then_inc(side_cp, 1)

            def hidden_lo(step, i):
                dve.wait_ge(e_hi, step * NBLK + (i + 1))
                dve.tensor_tensor(hel[:, i % 2, :, :], ps[:, 4 + i % 2, 0:256].rearrange("p (f s) -> p f s", s=P),
                                  heh[:, i % 2, :, :].bitcast(F32), ALU.subtract).then_inc(e_lo, 1)

            one_hot(0)
            for n in range(AHEAD):
                lo_moe(0, n)
            for c in range(4):
                gathered_lo(0, c)
            dve.wait_ge(side_cp, 4)
            dve.tensor_copy(xel[:, :, :], xnl[:, :, :].bitcast(F32)).then_inc(xel_ok, 1)
            slots_copy(0)
            dve.wait_ge(rt_total, 1)
            total = dve.value_load(total_i[0:1, 0:1], min_val=NE, max_val=ROUNDS * NE)
            with dve.Fori(0, total) as step:
                for n, (kind, i) in enumerate(EXPERT):
                    if (kind, i) == ("d", NBLK - 2):
                        hidden_lo(step, NBLK - 1)
                        dve.wait_ge(unit_done, step * NX + (N_DENSE + n))
                        dve.wait_ge(side_cp, step * 14 + 18)
                        dve.tensor_copy(xel[:, :, :], xnl[:, :, :].bitcast(F32)).then_inc(xel_ok, 1)
                    lo_moe(step, n + AHEAD)
                    if kind == "a" and i >= 1:
                        hidden_lo(step, i - 1)
                    if kind == "b":
                        dve.wait_ge(e_silu, step * NBLK + (i + 1))
                        dve.tensor_tensor(hf[:, i % 2, :], sil[:, i % 2, :], ps[:, 2 + i % 2, 256:512], ALU.mult).then_inc(e_h, 1)
                        if i == NBLK // 2 - 1:
                            one_hot(step + 1)
                    if n in SIDE:
                        what, arg = SIDE[n]
                        if what == "scatter":
                            add_back(step * 14 + 6, arg)
                            if arg[1] == KD - 1:
                                dve.tensor_copy(slot_cur[:, :], slot_next[:, :])
                                dve.tensor_copy(gs_cur[:, :], gs_next[:, :]).then_inc(slot_ok, 1)
                        elif what == "gather":
                            gathered_lo(step * 4 + 4, arg)
                        else:
                            slots_copy(step * 14 + 14)
                    if kind == "d" and i == NBLK - 1:
                        dve.wait_ge(y_hi, step + 1)
                        dve.scalar_tensor_tensor(ygl[:, :], ps[:, 0:2, :].rearrange("p b n -> p (b n)"), gs_cur[:, 0:1],
                                                 ygh[:, :].bitcast(F32), ALU.mult, ALU.subtract).then_inc(y_lo, 1)
            add_back(total * 14 + 6, range(KD))
            layer_norm(3, False)
            for k in range(6):
                t, half = k // 2, k % 2
                tn = TILES[t][1]
                dve.wait_ge(fin_tr, k + 1)
                dve.tensor_copy(yout[0:tn, t, 512 * half:512 * half + 512], ps[0:tn, FIN_BANK[k], :]).then_inc(fin_cp, 1)

        @block.tensor
        def _(pe):
            def product(out, wh, wl, ah, al, first, last):
                pe.matmul(out, wh, ah, start=first, stop=False)
                pe.matmul(out, wl, ah, start=False, stop=False)
                return pe.matmul(out, wh, al, start=False, stop=last)

            def weights(n):
                pe.wait_ge(lo_done, n + 1)
                return high[n % HI_RING], low[n % RING]

            def start_part(k):
                bank, t, f0 = START[k]
                if k >= FIRST_STARTS:
                    pe.wait_ge(start_lo, k - FIRST_STARTS + 2)
                tn = TILES[t][1]
                stage = mstage if k < MEM_STARTS else xstage
                for f in range(4):
                    last = pe.transpose(ps[:, bank, 128 * f:128 * f + tn],
                                        stage[0:tn, t, 128 * (f0 + f):128 * (f0 + f) + 128], ident[0:tn, 0:tn])
                last.then_inc(start_tr, 1)

            pe.wait_ge(const, 1)
            pe.wait_ge(ld_mem, 2 * 16)
            for k in range(MEM_STARTS):
                start_part(k)
            for n in range(4):
                if n == 0:
                    pe.wait_ge(ld_x, 3 * 16)
                    for k in range(MEM_STARTS, FIRST_STARTS):
                        start_part(k)
                    pe.wait_ge(start_lo, MEM_STARTS)
                wh, wl = weights(n)
                if n >= 2:
                    pe.wait_ge(mem_cp, n - 1)
                bank = 3 if n % 2 == 0 else 6
                for t in range(2):
                    for k in range(KD):
                        c = slice(256 * k, 256 * k + 256)
                        tok = slice(128 * t, 128 * t + 128)
                        out = ps[:, bank, 256 * t:256 * t + 256]
                        pe.matmul(out, mTh[:, k, tok], wh[:, c], start=k == 0, stop=False)
                        pe.matmul(out, mTl[:, k, tok], wh[:, c], start=False, stop=False)
                        last = pe.matmul(out, mTh[:, k, tok], wl[:, c], start=False, stop=k == KD - 1)
                last.then_inc(unit_done, 1)
                if n == 0:
                    for k in range(FIRST_STARTS, len(START)):
                        start_part(k)
                if n == 3:
                    pe.wait_ge(ld_vec, 5 * 16)
                    pe.wait_ge(start_lo, MEM_STARTS + 1)
                    pe.transpose(ps[:, 2, 0:76], vstage[:, :], ident[0:76, 0:76]).then_inc(start_tr, 1)
                if n % 2 == 1:
                    l = n // 2
                    pe.wait_ge(mem_cp, 2 * l + 1)
                    pe.wait_ge(start_lo, len(START))
                    for p in range(2):
                        for t in range(2):
                            last = pe.transpose(ps[:, 4 + l, 256 * p + 128 * t:256 * p + 128 * t + 128],
                                                mtok[:, l, t, 128 * p:128 * p + 128], ident[:, :])
                    last.then_inc(mkT_tr, 1)

            def event(l, e):
                kind, g, r = e
                no = l * N_EVENTS + EVENT_NO[e]
                if no >= 1:
                    pe.wait_ge(tr_cp, no)
                if kind == "memk":
                    if r == 0:
                        pe.wait_ge(ld_memk, 16 * (2 * l + g + 1))
                    for b in range(2):
                        for p in range(2):
                            for t in range(2):
                                last = pe.transpose(ps_tr[:, b, 256 * p + 128 * t:256 * p + 128 * t + 128],
                                                    kstage[:, 2 * r + b, t, 128 * p:128 * p + 128], ident[:, :])
                elif kind == "kvtok":
                    pe.wait_ge(z_cp, l * 38 + 8)
                    pe.wait_ge(ld_conv, 16 * (l + 1))
                    for i in range(2):
                        for t, (t0, tn) in enumerate(TILES):
                            pe.transpose(ps_tr[0:tn, i, 128 * t:128 * t + 128], kvT[:, i, t0:t0 + tn], ident[:, :])
                    for f in range(2):
                        last = pe.transpose(ps_tr[:, 0, 384 + 16 * f:400 + 16 * f],
                                            ustage[0:16, 128 * f:128 * f + 128], ident[0:16, 0:16])
                elif kind == "conv":
                    pe.wait_ge(ulast_done, l + 1)
                    for f in range(2):
                        last = pe.transpose(ps_tr[0:18, 0, 128 * f:128 * f + 128], ulast[:, f, :], ident[:, :])
                elif kind == "wink":
                    pe.wait_ge(ld_wink, 16 * (l + 1))
                    for b in range(NB):
                        last = pe.transpose(ps_tr[:, b // 4, 128 * (b % 4):128 * (b % 4) + 128], wstage[:, b, :], ident[:, :])
                else:
                    pe.wait_ge(probs, l * NJ + g + 1)
                    jk, ji = JOBS[g]
                    n, w = job_shape(jk, ji)
                    for s in range(n):
                        if jk == "swin":
                            pe.transpose(ps_tr[:, 0, 128 * s:128 * s + 128], sc[:, s, 0:128], ident[:, :])
                            last = pe.transpose(ps_tr[0:64, 1, 128 * s:128 * s + 128], sc[:, s, 128:192], ident[:, :])
                        else:
                            for kb in range(w // 128):
                                last = pe.transpose(ps_tr[:, kb, 128 * s:128 * s + 128],
                                                    sc[:, s, 128 * kb:128 * kb + 128], ident[:, :])
                last.then_inc(tr_mm, 1)

            def scores(l, j):
                kind, idx = JOBS[j]
                if l * NJ + j >= 1:
                    pe.wait_ge(exp_done, l * NJ + j)
                if j == 0:
                    pe.wait_ge(z_cp, l * 38 + 2)
                if kind == "smem":
                    pe.wait_ge(tr_cp, l * N_EVENTS + EVENT_NO[("memk", idx, 1)] + 1)
                    for b in range(4):
                        for p in range(2):
                            last = pe.matmul(ps_sc[32 * b:32 * b + 32, 0, :], qm_diag[:, p, 4 * idx + b, :],
                                             mem_kT[:, b, p, :], start=p == 0, stop=p == 1)
                elif kind == "pmem":
                    pe.wait_ge(mkT_cp, l + 1)
                    for s, h in enumerate(SEGMENT_HEADS):
                        r = slice(64 * (h % 2), 64 * (h % 2) + 64)
                        last = pe.matmul(ps_sc[:, s, :], qmT[r, h // 2, 128 * idx:128 * idx + 128],
                                         mkT[r, l, h // 2, :], start=True, stop=True)
                elif kind == "pwin":
                    n, kv = idx
                    r = slice(64 * kv, 64 * kv + 64)
                    for g in range(4):
                        last = pe.matmul(ps_sc[:, g, 0:128 * (n + 1)], qT[r, g, 128 * n:128 * n + 128],
                                         kvT[r, 0, 0:128 * (n + 1)], start=True, stop=True)
                else:
                    pe.wait_ge(tr_cp, l * N_EVENTS + EVENT_NO[("wink", 0, 0)] + 1)
                    for kv in range(2):
                        r = slice(64 * kv, 64 * kv + 64)
                        for bg in range(2):
                            for b in range(4):
                                seq = 4 * bg + b
                                q = qS[r, seq, :, :].rearrange("p g t -> p (g t)")
                                out = ps_sc[32 * b:32 * b + 32, 2 * kv + bg, :]
                                pe.matmul(out[:, 0:128], q, win_kT[r, seq, :], start=True, stop=True)
                                last = pe.matmul(out[:, 128:192], q, kvT[r, 0, NP:T], start=True, stop=True)
                last.then_inc(sc_mm, 1)

            def values(l, j):
                kind, idx = JOBS[j]
                pe.wait_ge(tr_cp, l * N_EVENTS + EVENT_NO[("probs", j, 0)] + 1)
                if l * NJ + j >= 1:
                    pe.wait_ge(o_lo, l * NJ + j)
                if kind == "smem":
                    pe.wait_ge(ld_memv, 16 * (2 * l + idx + 1))
                    for b in range(4):
                        for p in range(2):
                            c = 128 * p + 32 * b
                            for t in range(2):
                                last = pe.matmul(ps[:, 3, c:c + 32], mem_v[:, b, t, 128 * p:128 * p + 128],
                                                 pT[:, t, 32 * b:32 * b + 32], start=t == 0, stop=t == 1)
                elif kind == "pmem":
                    pe.wait_ge(mem_cp, 2 * l + 2)
                    for s, h in enumerate(SEGMENT_HEADS):
                        out = ps[64 * (h % 2):64 * (h % 2) + 64, 3, 128 * (h // 2):128 * (h // 2) + 128]
                        for t in range(2):
                            last = pe.matmul(out, mv[:, l, t, 64 * h:64 * h + 64], pT[:, t, 128 * s:128 * s + 128],
                                             start=t == 0, stop=t == 1)
                elif kind == "pwin":
                    n, kv = idx
                    for t in range(n + 1):
                        last = pe.matmul(ps[64 * kv:64 * kv + 64, 3, :], kvtok[:, 1, t, 64 * kv:64 * kv + 64],
                                         pT[:, t, :], start=t == 0, stop=t == n)
                else:
                    pe.wait_ge(ld_winv, 16 * (l + 1))
                    pe.matmul(ps[:, 3, :], kvtok[0:64, 1, 2, :], pT[0:64, 1, :], start=True, stop=False)
                    out = ps[:, 3, :].rearrange("p (v c) -> p v c", c=256)
                    cached = pT[:, 0, :].rearrange("p (v c) -> p v c", c=256)
                    for b in range(NB):
                        last = pe.matmul(out[:, :, 32 * b:32 * b + 32], win_v[:, b, :], cached[:, :, 32 * b:32 * b + 32],
                                         start=False, stop=b == NB - 1)
                last.then_inc(pv_mm, 1)

            def free_bank(l, q):
                if q < 3:
                    return
                kind, f = OUTS[q - 3]
                if kind == "z":
                    pe.wait_ge(z_cp, l * 38 + f + 1)
                elif kind == "wo":
                    pe.wait_ge(resid, 16 * l + f + 1)
                else:
                    pe.wait_ge(merge_done, l * len(MERGES) + MERGE_NO[(kind, f)] + 1)

            def mixer(l):
                for i, u in enumerate(layer_units(l)):
                    n = UNIT_OF[u]
                    wh, wl = weights(n)
                    if u[0] in ("z", "wo"):
                        tiles, kn, width = [(u[0], 2 * u[2]), (u[0], 2 * u[2] + 1)], KD, 256
                        ah, al = xh, xl
                    elif u[0] == "pattn":
                        tiles, kn, width = [("pattn", 4 * u[2] + f) for f in range(4)], 4, 512
                        ah, al = oah, oal
                        pe.wait_ge(o_lo, l * NJ + NJ)
                    else:
                        tiles, kn, width = [(u[0], f) for f in range(KD)], 2, D
                        ah, al = (och, ocl) if u[0] == "pconv" else (omh, oml)
                        if u[0] == "pconv":
                            pe.wait_ge(ocl_done, l + 1)
                        else:
                            pe.wait_ge(o_lo, l * NJ + 4)
                    if i == 0:
                        for k in range(KD):
                            if l == 1:
                                pe.wait_ge(xl_done, KD + k + 1)
                            for m in range(2):
                                c = slice(256 * k + 128 * m, 256 * k + 128 * m + 128)
                                last = product(ps[:, (l * len(OUTS) + m) % 3, 0:T], wh[:, c], wl[:, c],
                                               xh[:, k, :], xl[:, k, :], k == 0, k == KD - 1)
                                if m == 0 and k == KD - 1:
                                    last.then_inc(out_mm, 1)
                    for m, tile in enumerate(tiles if i else ()):
                        q = OUT_NO[tile]
                        free_bank(l, q)
                        for k in range(kn):
                            if u == ("wo", l, 0) and m == 0:
                                pe.wait_ge(ml_done, KD * l + k + 1)
                            c = slice(width * k + 128 * m, width * k + 128 * m + 128)
                            last = product(ps[:, (l * len(OUTS) + q) % 3, 0:T], wh[:, c], wl[:, c],
                                           ah[:, k, :], al[:, k, :], k == 0, k == kn - 1)
                        if m < len(tiles) - 1:
                            last.then_inc(out_mm, 1)
                    last.then_inc(unit_done, 1)
                    for work in SLOTS.get(i, ()):
                        if work[0] == "pv":
                            values(l, work[1])
                        elif work[0] == "event":
                            event(l, work[1:])
                        else:
                            scores(l, work[1])

            def layer_norm(L, base, order):
                for k, f in enumerate(order):
                    if base is None:
                        pe.wait_ge(resid, KD * L + k + 1)
                    last = pe.matmul(ps[:, MEAN, 0:T], mean_of[:, :], x[:, f, :], start=k == 0, stop=k == KD - 1)
                last.then_inc(mean_mm, 1)
                sq = sq_last if L == 3 else sq_dense
                for f in range(KD):
                    pe.wait_ge(squared, KD * L + f + 1)
                    pe.matmul(ps[:, VAR, 0:T], mean_of[:, :], sq[:, f, :], start=f == 0, stop=f == KD - 1
                              ).then_inc(var_mm, 1)

            DOWN = (4, 5, 6, 7, 0, 1, 2, 3)
            pe.wait_ge(vconst, 1)
            pe.wait_ge(const, CONSTS)
            mixer(0)
            layer_norm(0, None, range(KD))
            for i in range(NBLK):
                for half, kind in enumerate(("fg", "fu")):
                    n = UNIT_OF[(kind, 0, i)]
                    wh, wl = weights(n)
                    if i >= 2 and half == 0:
                        pe.wait_ge(ff_h, i - 1)
                    order = [(m, k) for m in range(2) for k in range(KD)]
                    if i == 0 and half == 0:
                        order.sort(key=lambda mk: mk[1])
                    for m, k in order:
                        if i == 0 and half == 0 and m == 0:
                            pe.wait_ge(xl_done, k + 1)
                        c = slice(256 * k + 128 * m, 256 * k + 128 * m + 128)
                        last = product(ps[:, 4 * (i % 2) + 2 * half + m, 0:T], wh[:, c], wl[:, c],
                                       xh[:, k, :], xl[:, k, :], k == 0, k == KD - 1)
                    last.then_inc(unit_done, 1)
            for i in range(NBLK):
                n = UNIT_OF[("fd", 0, i)]
                wh, wl = weights(n)
                pe.wait_ge(ff_lo, i + 1)
                for k in range(2):
                    for f in DOWN:
                        if i == 0 and k == 0 and f in (4, 0):
                            pe.wait_ge(ff_h, NBLK - 1 if f == 4 else NBLK)
                        c = slice(D * k + 128 * f, D * k + 128 * f + 128)
                        last = product(ps[:, f, 0:T], wh[:, c], wl[:, c], hTh[:, 2 * i + k, :], hTl[:, 2 * i + k, :],
                                       i == 0 and k == 0, i == NBLK - 1 and k == 1)
                        if i == NBLK - 1 and k == 1 and f != DOWN[-1]:
                            last.then_inc(down_mm, 1)
                last.then_inc(unit_done, 1)
            layer_norm(1, None, DOWN)
            mixer(1)
            layer_norm(2, None, range(KD))

            pe.wait_ge(x_done, KD * 3)
            pe.wait_ge(ld_const, CONST_LOADS + 32)
            for t, (t0, tn) in enumerate(TILES):
                for k in range(KD):
                    last = pe.matmul(ps[0:tn, 0, 8 * t:8 * t + 8], x[:, k, t0:t0 + tn], rw[:, k, :],
                                     start=k == 0, stop=k == KD - 1)
            last.then_inc(rt_mm, 1)
            for k in range(6):
                t0, tn = TILES[k // 2]
                for f in range(4):
                    last = pe.transpose(ps[0:tn, 2 + k, 128 * f:128 * f + 128], x[:, 4 * (k % 2) + f, t0:t0 + tn], ident[:, :])
                last.then_inc(xt_mm, 1)
            pe.wait_ge(rt_sel, 3)
            pe.wait_ge(const, CONSTS + 1)
            for t, (t0, tn) in enumerate(TILES):
                for m in range(t):
                    pe.matmul(ps[0:tn, 1, 8 * t:8 * t + 8], ones[:, 0:tn], chosen[:, m, :], start=m == 0, stop=False)
                pe.matmul(ps[0:tn, 1, 8 * t:8 * t + 8], before[0:tn, 0:tn], chosen[0:tn, t, :], start=t == 0, stop=True)
            for t, (t0, tn) in enumerate(TILES):
                last = pe.matmul(ps[:, 1, 24:32], ones[0:tn, :], chosen[0:tn, t, :], start=t == 0, stop=t == 2)
            last.then_inc(rt_rank, 1)

            def gather(first, c, prologue=False):
                if not (prologue and c < 2):
                    pe.wait_ge(side_cp, first + (c - 1))
                for part, tok in enumerate((xtokh, xtokl)):
                    for f in range(2):
                        out = ps[:, 6 + c % 2, 256 * part + 128 * f:256 * part + 128 * f + 128]
                        for t, (t0, tn) in enumerate(TILES):
                            cols = slice(128 * (2 * c + f), 128 * (2 * c + f) + 128)
                            last = pe.matmul(out, tok[0:tn, t, cols], onehot[0:tn, t, :], start=t == 0, stop=t == 2)
                last.then_inc(side_mm, 1)

            def slots_and_gates(first):
                pe.wait_ge(side_cp, first + 3)
                for t, (t0, tn) in enumerate(TILES):
                    last = pe.transpose(ps[:, 6, t0:t0 + tn], onehot[0:tn, t, :].bitcast(F32), ident[0:tn, 0:tn])
                last.then_inc(side_mm, 1)
                pe.wait_ge(side_cp, first + 4)
                for t, (t0, tn) in enumerate(TILES):
                    last = pe.matmul(ps[:, 7, 0:1], onehot[0:tn, t, :].bitcast(F32), gcol[0:tn, t:t + 1], start=t == 0, stop=t == 2)
                last.then_inc(side_mm, 1)

            def scatter(first, tiles):
                for f in tiles:
                    pe.wait_ge(side_cp, first + (f - 1))
                    cols = slice(128 * f, 128 * f + 128)
                    out = ps[:, 6 + f % 2, 0:T]
                    pe.matmul(out, ygh[:, cols], slot_cur[:, :], start=True, stop=False)
                    pe.matmul(out, ygl[:, cols], slot_cur[:, :], start=False, stop=True).then_inc(side_mm, 1)

            pe.wait_ge(xt_lo, 6)
            pe.wait_ge(oh_done, 1)
            for c in range(4):
                gather(0, c, prologue=True)
            slots_and_gates(0)
            pe.wait_ge(rt_total, 1)
            total = pe.value_load(total_i[0:1, 0:1], min_val=NE, max_val=ROUNDS * NE)
            with pe.Fori(0, total) as step:
                def block_transposed(i):
                    pe.wait_ge(e_h, step * NBLK + (i + 1))
                    for f in range(2):
                        last = pe.transpose(ps[:, 4 + i % 2, 128 * f:128 * f + 128], hf[:, i % 2, 128 * f:128 * f + 128], ident[:, :])
                    last.then_inc(e_tr, 1)

                for n, (kind, i) in enumerate(EXPERT):
                    pe.wait_ge(lo_done, step * NX + (N_DENSE + n + 1))
                    wh, wl = high[(N_DENSE + n) % HI_RING], low_moe[n % RING_MOE]
                    if kind == "d":
                        pe.wait_ge(e_lo, step * NBLK + (i + 1))
                        if i == 0:
                            pe.wait_ge(y_lo, step + 1)
                        for k in range(2):
                            if k == 1 and i == NBLK - 2:
                                block_transposed(NBLK - 1)
                            for half in range(2):
                                c = slice(D * k + 512 * half, D * k + 512 * half + 512)
                                out = ps[:, half, :]
                                pe.matmul(out, heh[:, i % 2, k, :], wh[:, c], start=i == 0 and k == 0, stop=False)
                                pe.matmul(out, heh[:, i % 2, k, :], wl[:, c], start=False, stop=False)
                                last = pe.matmul(out, hel[:, i % 2, k, :], wh[:, c], start=False,
                                                 stop=i == NBLK - 1 and k == 1)
                        last.then_inc(unit_done, 1)
                        continue
                    if kind == "a":
                        if i == 0:
                            pe.wait_ge(xe_ok, step + 1)
                            pe.wait_ge(xel_ok, step + 1)
                        if i >= 2:
                            pe.wait_ge(e_h, step * NBLK + (i - 1))
                    k0 = 0 if kind == "a" else KD // 2
                    for k in range(KD // 2):
                        c = slice(512 * k, 512 * k + 512)
                        pe.matmul(ps[:, 2 + i % 2, :], xeh[:, k0 + k, :], wh[:, c], start=k0 + k == 0, stop=False)
                        pe.matmul(ps[:, 2 + i % 2, :], xeh[:, k0 + k, :], wl[:, c], start=False, stop=False)
                        last = pe.matmul(ps[:, 2 + i % 2, :], xel[:, k0 + k, :], wh[:, c], start=False, stop=k0 + k == KD - 1)
                    last.then_inc(unit_done, 1)
                    if kind == "a" and i >= 1:
                        block_transposed(i - 1)
                    if n in SIDE:
                        what, arg = SIDE[n]
                        if what == "scatter":
                            if arg[0] == 0:
                                pe.wait_ge(slot_ok, step + 1)
                                pe.wait_ge(y_lo, step + 1)
                            scatter(step * 14 + 6, arg)
                        elif what == "gather":
                            if arg == 0:
                                pe.wait_ge(oh_done, step + 2)
                            gather(step * 14 + 14, arg)
                        else:
                            slots_and_gates(step * 14 + 14)
            pe.wait_ge(slot_ok, total + 1)
            pe.wait_ge(y_lo, total + 1)
            scatter(total * 14 + 6, range(KD))
            pe.wait_ge(side_cp, total * 14 + 14)
            layer_norm(3, 1, range(KD))
            for k in range(6):
                t0, tn = TILES[k // 2]
                if k == 0:
                    pe.wait_ge(x_done, KD * 4)
                for f in range(4):
                    last = pe.transpose(ps[0:tn, FIN_BANK[k], 128 * f:128 * f + 128],
                                        x[:, 4 * (k % 2) + f, t0:t0 + tn], ident[:, :])
                last.then_inc(fin_tr, 1)


_INS = ["x_prompt", "x_sample", "mem_prompt", "cache_win_k", "cache_win_v", "cache_conv", "cache_mem_k",
        "cache_mem_v", "w_in", "conv_w", "sink", "p_attn", "p_conv", "p_mem", "w_o", "w_mem_k", "w_mem_v",
        "ln1_g", "ln1_b", "ln2_g", "ln2_b", "ffn_w_gate", "ffn_w_up", "ffn_w_down", "router_w", "router_b",
        "exp_w_gate", "exp_w_up", "exp_w_down"]
_OUTS = [("y_prompt", (1, 256, 1024)), ("y_sample", (8, 8, 1024)),
         ("win_k_prompt", (2, 1, 128, 2, 64)), ("win_v_prompt", (2, 1, 128, 2, 64)),
         ("conv_prompt", (2, 1, 2, 256)),
         ("mem_k_prompt", (2, 1, 256, 4, 64)), ("mem_v_prompt", (2, 1, 256, 4, 64)),
         ("win_k_sample", (2, 8, 128, 2, 64)), ("win_v_sample", (2, 8, 128, 2, 64)),
         ("conv_sample", (2, 8, 2, 256))]


def kernel(**inputs):
    import numpy as _np
    import concourse.bacc as _bacc
    from concourse import mybir as _mybir
    from concourse.bass_utils import run_bass_kernel_spmd as _run

    nc = _bacc.Bacc("TRN2", target_bir_lowering=False, num_devices=1)
    arrays, A, O = {}, {}, {}
    for name in _INS:
        a = _np.ascontiguousarray(inputs[name])
        arrays[f"in_{name}_dram"] = a
        A[name] = nc.dram_tensor(f"in_{name}_dram", a.shape, _mybir.dt.from_np(a.dtype), kind="ExternalInput").ap()
    for name, shape in _OUTS:
        O[name] = nc.dram_tensor(f"out_{name}_dram", shape, _mybir.dt.float32, kind="ExternalOutput").ap()
    build_trunk(nc, A, O)
    r = _run(nc, [arrays], core_ids=[0])
    return tuple(r.results[0][f"out_{name}_dram"] for name, _ in _OUTS)
```

```python
from contextlib import ExitStack

import concourse.bass as bass
from concourse import mybir

F32 = mybir.dt.float32
F32R = mybir.dt.float32r
I32 = mybir.dt.int32
U32 = mybir.dt.uint32
ALU = mybir.AluOpType
ACT = mybir.ActivationFunctionType
AX = mybir.AxisListType.X

P = 128
D = 1024
KD = D // P
NP = 256
NB = 8
TS = 8
NS = NB * TS
T = NP + NS
HD = 64
NEG = -1.0e30
SCALE = HD ** -0.5
ALPHA = 4 ** 0.25
EPS = 1e-5
FF = 2816
NBLK = FF // 256
NE = 8
ROUNDS = 3

UNIT = 2048
RING = 6
HI_RING = 3
HALVES = (slice(0, UNIT // 2), slice(UNIT // 2, UNIT))
RING_MOE = 11
AHEAD = HI_RING - 1

FIN_BANK = (0, 1, 2, 3, 6, 7)
XT_BANK = (3, 6, 7, 4, 5, 3)
TILES = ((0, 128), (128, 128), (256, 64))

Z_COLS = ([1536, 0, 256, 512, 768, 1024, 1280]
          + [2816 + 256 * i for i in range(4)]
          + [3840 + 256 * i for i in range(4)]
          + [1792 + 256 * i for i in range(4)])


def layer_units(l):
    z = [("z", l, i) for i in range(19)]
    return (z[0:11] + [("pconv", l, 0)] + z[11:15] + [("pmem", l, 0)] + z[15:19]
            + [("pattn", l, i) for i in range(2)] + [("wo", l, i) for i in range(4)])


def ffn_units():
    return [(k, 0, i) for i in range(NBLK) for k in ("fg", "fu")] + [("fd", 0, i) for i in range(NBLK)]


STREAM = ([(k, l, 0) for l in range(2) for k in ("mk", "mv")]
          + layer_units(0) + ffn_units() + layer_units(1))
N_DENSE = len(STREAM)
UNIT_OF = {u: n for n, u in enumerate(STREAM)}
EXPERT = [("a", 0), ("b", 0)]
for _i in range(1, NBLK):
    EXPERT += [("a", _i), ("b", _i), ("d", _i - 1)]
EXPERT += [("d", NBLK - 1)]
NX = len(EXPERT)
assert NX % RING_MOE == 0 and NX % HI_RING == 0
LDX_VALUE, _at = [], [0] * RING_MOE
for _n, (_k, _) in enumerate(EXPERT):
    _at[_n % RING_MOE] += 16 if _k == "d" else 32
    LDX_VALUE.append(_at[_n % RING_MOE])
LDX_STEP = list(_at)
SIDE = {EXPERT.index(u): ("scatter", (2 * c, 2 * c + 1))
        for c, u in enumerate((("b", 1), ("b", 2), ("b", 3), ("b", 4)))}
SIDE.update({EXPERT.index(("b", NBLK - 6 + c)): ("gather", c) for c in range(4)})
SIDE[EXPERT.index(("b", NBLK - 2))] = ("slots", 0)

LD_VALUE, _at = [], [0] * RING_MOE
for _n, _u in enumerate(STREAM):
    _at[_n % RING] += 32 if _u[0] == "pattn" else 16
    LD_VALUE.append(_at[_n % RING])
LD_BASE = list(_at)

JOBS = [("pmem", 0), ("pmem", 1), ("smem", 0), ("smem", 1),
        ("pwin", (0, 0)), ("pwin", (0, 1)), ("pwin", (1, 0)), ("pwin", (1, 1)), ("swin", 0)]
NJ = len(JOBS)
SEGMENT_HEADS = (0, 2, 1, 3)


def job_shape(kind, idx):
    if kind == "smem":
        return 1, 256
    if kind == "pmem":
        return 4, 256
    if kind == "pwin":
        return 4, 128 * (idx[0] + 1)
    return 4, 192


def beside_units():
    after = {0: [("event", "memk", 0, 0)], 1: [], 3: []}
    for j in range(NJ):
        for lag, work in ((0, ("scores", j)), (2, ("event", "probs", j, 0)), (3, ("pv", j))):
            after.setdefault(2 * j + lag, []).append(work)
    after[1].append(("event", "memk", 0, 1))
    after[4] += [("event", "kvtok", 0, 0), ("event", "memk", 1, 0)]
    after[5].append(("event", "memk", 1, 1))
    after[8].append(("event", "wink", 0, 0))
    after[9].append(("event", "conv", 0, 0))
    order = {"pv": 0, "event": 1, "scores": 2}
    for w in after:
        after[w].sort(key=lambda x: 3 if x[0] == "event" and x[1] != "probs" else order[x[0]])
    return after


SLOTS = beside_units()
EVENTS = [x[1:] for w in sorted(SLOTS) for x in SLOTS[w] if x[0] == "event"]
N_EVENTS = len(EVENTS)
EVENT_NO = {e: n for n, e in enumerate(EVENTS)}

OUTS = []
for _u in layer_units(0):
    if _u[0] == "z":
        OUTS += [("z", 2 * _u[2]), ("z", 2 * _u[2] + 1)]
    elif _u[0] in ("pconv", "pmem"):
        OUTS += [(_u[0], f) for f in range(KD)]
    elif _u[0] == "pattn":
        OUTS += [("pattn", 4 * _u[2] + f) for f in range(4)]
    else:
        OUTS += [("wo", 2 * _u[2]), ("wo", 2 * _u[2] + 1)]
OUT_NO = {o: n for n, o in enumerate(OUTS)}
OUT_SIGNAL, _mid = {}, 0
for _k, _u in enumerate(layer_units(0)):
    _n = {"z": 2, "wo": 2, "pattn": 4, "pconv": KD, "pmem": KD}[_u[0]]
    for _m in range(_n):
        _mid += _m < _n - 1
        OUT_SIGNAL[OUTS[len(OUT_SIGNAL)]] = (_k, _m == _n - 1, _mid)
OUT_MIDS = _mid
MERGES = [o for o in OUTS if o[0] in ("pconv", "pmem", "pattn")]
MERGE_NO = {o: n for n, o in enumerate(MERGES)}


def build_trunk(nc, A, O):
    with ExitStack() as ctx:
        base = (nc.sbuf_base + 63) // 64 * 64
        end = nc.sbuf_usable_end
        place = {"at": base}

        def at(name, shape, dt, offset):
            words = 1
            for s in shape[1:]:
                words *= s
            assert offset + 4 * words <= end, (name, offset + 4 * words - end)
            return nc.alloc_sbuf_tensor_at(name, shape, dt, offset=offset)

        def take(name, shape, dt=F32):
            words = 1
            for s in shape[1:]:
                words *= s
            t = at(name, shape, dt, place["at"])
            place["at"] += (4 * words + 31) // 32 * 32
            return t

        def sem(name):
            return ctx.enter_context(nc.semaphore(name))

        ring_at = place["at"]
        raw = [at(f"raw{s}", [P, UNIT], F32, ring_at + 4 * UNIT * s) for s in range(RING)]
        low = [at(f"low{s}", [P, UNIT], F32R, ring_at + 4 * UNIT * s) for s in range(RING)]
        place["at"] = ring_at + 4 * UNIT * RING
        high = [take(f"high{s}", [P, UNIT], F32R) for s in range(HI_RING)]

        x = take("x", [P, KD, T])
        ident = take("ident", [P, P])
        mean_of = take("mean_of", [P, P])
        mask_win = take("mask_win", [P, 256])
        mask_dec = take("mask_dec", [P, 2, 192])
        vecs = take("vecs", [P, 76])
        sink_p = take("sink_p", [P, 2, 8])
        sink_s = take("sink_s", [P, 2, 2])
        small = take("small", [P, 64])
        eps = take("eps", [P, 1])
        std = take("std", [P, T])
        iota_i = at("iota_i", [P, P], I32, place["at"] - 4 * T)
        ulast = take("ulast", [P, 2, 18])
        uout = take("uout", [18, 256])
        iota_f = take("iota_f", [P, P])
        row_i = take("row_i", [P, 4], I32)
        row_f = take("row_f", [P, 4])
        scratch_at = place["at"]

        xh = take("xh", [P, KD, T], F32R)
        xl = take("xl", [P, KD, T], F32R)
        mkT = take("mkT", [P, 2, 2, 256])
        mv = take("mv", [P, 2, 2, 256])
        mix_at = place["at"]
        gate = take("gate", [P, KD, T])
        sq_dense = at("sq_dense", [P, KD, T], F32, mix_at)
        merged = take("merged", [P, KD, T])
        hbc = at("hbc", [P, 6, T], F32, place["at"] - 4 * KD * T)
        qT = take("qT", [P, 4, NP])
        qS = take("qS", [P, NB, 4, TS])
        qmT = take("qmT", [P, 2, NP])
        qm_diag = take("qm_diag", [P, 2, NB, 32])
        kvT = take("kvT", [P, 2, T])
        uext = take("uext", [P, 2, NP + 2 + NB * (TS + 2)])
        sc = take("sc", [P, 4, 256])
        pT = take("pT", [P, 2, 512])
        oah = take("oah", [P, 4, T], F32R)
        oal = take("oal", [P, 4, T], F32R)
        omh = take("omh", [P, 2, T], F32R)
        oml = take("oml", [P, 2, T], F32R)
        och = take("och", [P, 2, T], F32R)
        ocl = take("ocl", [P, 2, T], F32R)
        kvtok = take("kvtok", [P, 2, 3, P])
        kstage = take("kstage", [P, 4, 2, 256])
        mem_kT_at = place["at"]
        mem_kT = take("mem_kT", [P, 4, 2, 256])
        win_kT = at("win_kT", [P, NB, P], F32, mem_kT_at)
        win_v = at("win_v", [P, NB, P], F32, mem_kT_at + 4096)
        mem_v = take("mem_v", [P, 4, 2, 256])
        ustage = at("ustage", [16, 256], F32, mix_at + 4 * 14 * T)
        wstage = at("wstage", [P, NB, P], F32, place["at"] - 4 * 3 * 2048)

        xstage = at("xstage", [P, 3, D], F32, mix_at)
        mstage = at("mstage", [P, 2, D], F32, mix_at + 12288)
        mTh = at("mTh", [P, KD, NP], F32R, mix_at + 20480)
        mTl = at("mTl", [P, KD, NP], F32R, mix_at + 28672)
        mtok = at("mtok", [P, 2, 2, 256], F32, mix_at + 36864)
        vstage = at("vstage", [76, P], F32, mix_at + 40960)

        hTh = at("hTh", [P, 22, T], F32R, mix_at)
        hTl = at("hTl", [P, 22, T], F32R, mix_at + 4 * 22 * T)
        silu = at("silu", [P, 2, 2, T], F32, mix_at + 8 * 22 * T)
        hfull = at("hfull", [P, 2, 2, T], F32, mix_at + 8 * 22 * T + 16 * T)

        place["at"] = scratch_at
        xtok = take("xtok", [P, 3, D])
        xeh = take("xeh", [P, KD, P], F32R)
        xel = take("xel", [P, KD, P], F32R)
        xn = take("xn", [P, KD, P])
        ygh = take("ygh", [P, D], F32R)
        ygl = take("ygl", [P, D], F32R)
        sil = take("sil", [P, 2, 256])
        hf = take("hf", [P, 2, 256])
        heh = take("heh", [P, 2, 2, P], F32R)
        hel = take("hel", [P, 2, 2, P], F32R)
        onehot = take("onehot", [P, 3, P])
        slot_next = take("slot_next", [P, T], F32R)
        slot_cur = take("slot_cur", [P, T], F32R)
        gs_next = take("gs_next", [P, 1])
        gs_cur = take("gs_cur", [P, 1])
        gcol = take("gcol", [P, 3])
        rw = take("rw", [P, KD, NE])
        rb = take("rb", [P, NE])
        logit = take("logit", [P, 3, NE])
        top = take("top", [P, 3, 8])
        topi = take("topi", [P, 3, 8], U32)
        topf = take("topf", [P, 3, 8])
        pair = take("pair", [P, 3, 4])
        oh1 = take("oh1", [P, 3, NE])
        oh2 = take("oh2", [P, 3, NE])
        chosen = take("chosen", [P, 3, NE])
        gates = take("gates", [P, 3, ROUNDS * NE + 1])
        posm = take("posm", [P, 3, NE])
        pos = take("pos", [P, 3, ROUNDS * NE + 1])
        before = take("before", [P, P])
        ones = take("ones", [P, P])
        cnt = take("cnt", [P, 4])
        total_i = take("total_i", [P, 1], I32)
        sq_last = take("sq_last", [P, KD, T])
        yout = at("yout", [P, 3, D], F32, scratch_at)
        ext_at = end - 4 * UNIT * (RING_MOE - RING)
        ext_at -= ext_at % 64
        assert place["at"] <= ext_at, place["at"] - ext_at
        raw_moe = raw + [at(f"raw{s}", [P, UNIT], F32, ext_at + 4 * UNIT * (s - RING))
                         for s in range(RING, RING_MOE)]
        low_moe = low + [at(f"low{s}", [P, UNIT], F32R, ext_at + 4 * UNIT * (s - RING))
                         for s in range(RING, RING_MOE)]

        ps = ctx.enter_context(nc.psum_tensor("ps", [P, 8, 512], F32))
        ps_sc = ps[:, 4:6, :].rearrange("p b (s w) -> p (b s) w", w=256)
        ps_tr = ps[:, 6:8, :]
        MEAN, VAR = 4, 5

        ld = [sem(f"loaded{s}") for s in range(RING_MOE)]
        hi_done = sem("hi_done")
        lo_done = sem("lo_done")
        unit_done = sem("unit_done")
        zeroed = sem("zeroed")
        slot_ok = sem("slot_ok")
        ld_x = sem("ld_x")
        ld_mem = sem("ld_mem")
        ld_vec = sem("ld_vec")
        ld_const = sem("ld_const")
        const = sem("const")
        vconst = sem("vconst")
        start_tr = sem("start_tr")
        start_hi = sem("start_hi")
        start_lo = sem("start_lo")
        mem_cp = sem("mem_cp")
        mkT_tr = sem("mkT_tr")
        mkT_cp = sem("mkT_cp")
        out_mm = sem("out_mm")
        z_cp = sem("z_cp")
        conv_done = sem("conv_done")
        och_done = sem("och_done")
        ocl_done = sem("ocl_done")
        merge_done = sem("merge_done")
        mh_done = sem("mh_done")
        ml_done = sem("ml_done")
        sc_mm = sem("sc_mm")
        sc_cp = sem("sc_cp")
        exp_done = sem("exp_done")
        probs = sem("probs")
        tr_mm = sem("tr_mm")
        tr_cp = sem("tr_cp")
        pv_mm = sem("pv_mm")
        o_hi = sem("o_hi")
        o_lo = sem("o_lo")
        ulast_done = sem("ulast_done")
        ld_memk = sem("ld_memk")
        ld_memv = sem("ld_memv")
        ld_wink = sem("ld_wink")
        ld_winv = sem("ld_winv")
        ld_conv = sem("ld_conv")
        resid = sem("resid")
        mean_mm = sem("mean_mm")
        centered = sem("centered")
        squared = sem("squared")
        var_mm = sem("var_mm")
        std_done = sem("std_done")
        rstd_done = sem("rstd_done")
        normed = sem("normed")
        xh_done = sem("xh_done")
        x_new = sem("x_new")
        x_done = sem("x_done")
        xl_done = sem("xl_done")
        ff_silu = sem("ff_silu")
        ff_h = sem("ff_h")
        ff_hi = sem("ff_hi")
        ff_lo = sem("ff_lo")
        down_mm = sem("down_mm")
        rt_mm = sem("rt_mm")
        rt_top = sem("rt_top")
        rt_exp = sem("rt_exp")
        rt_sel = sem("rt_sel")
        rt_rank = sem("rt_rank")
        rt_total = sem("rt_total")
        xt_mm = sem("xt_mm")
        xt_cp = sem("xt_cp")
        x_scaled = sem("x_scaled")
        oh_done = sem("oh_done")
        side_mm = sem("side_mm")
        side_cp = sem("side_cp")
        xe_ok = sem("xe_ok")
        xel_ok = sem("xel_ok")
        xn_cp = sem("xn_cp")
        e_silu = sem("e_silu")
        e_h = sem("e_h")
        e_tr = sem("e_tr")
        e_hi = sem("e_hi")
        e_lo = sem("e_lo")
        y_hi = sem("y_hi")
        y_lo = sem("y_lo")
        fin_tr = sem("fin_tr")
        fin_cp = sem("fin_cp")
        fin_cp2 = sem("fin_cp2")
        chain = sem("chain")
        pchain = sem("pchain")
        dma_out = sem("dma_out")
        dma_y = sem("dma_y")
        dma_mid = sem("dma_mid")

        START = [(bank, k // 2, 4 * (k % 2)) for k, bank in enumerate((6, 7, 0, 1))]
        START += [(bank, k // 2, 4 * (k % 2)) for k, bank in enumerate((2, 4, 5, 7, 0, 1))]
        MEM_STARTS, FIRST_STARTS = 4, 7

        block = ctx.enter_context(nc.Block())

        def wait_out(eng, l, tile):
            unit, last, mids = OUT_SIGNAL[tile]
            if last:
                eng.wait_ge(unit_done, UNIT_OF[layer_units(l)[unit]] + 1)
            else:
                eng.wait_ge(out_mm, l * OUT_MIDS + mids)

        def attention_out(j):
            kind, idx = JOBS[j]
            if kind == "pmem":
                return [(omh, oml, lambda b: b[:, 0:2, 128 * idx:128 * idx + 128],
                         ps[:, 3, 0:256].rearrange("p (a t) -> p a t", t=128))]
            if kind == "pwin":
                n, kv = idx
                h = slice(64 * kv, 64 * kv + 64)
                return [(oah, oal, lambda b: b[h, :, 128 * n:128 * n + 128],
                         ps[h, 3, :].rearrange("p (g t) -> p g t", t=128))]
            parts = []
            if kind == "smem":
                for a in range(2):
                    for p in range(2):
                        h = slice(64 * a, 64 * a + 64)
                        src = ps[h, 3, 128 * p:128 * p + 128].rearrange("p (b c) -> p b c", c=32)[
                            :, :, (2 * p + a) * 8:(2 * p + a) * 8 + 8]
                        parts.append((omh, oml, lambda b, h=h, p=p: b[h, p, NP + 32 * idx:NP + 32 * idx + 32]
                                      .rearrange("p (b t) -> p b t", t=8), src))
                return parts
            for kv in range(2):
                h = slice(64 * kv, 64 * kv + 64)
                parts.append((oah, oal, lambda b, h=h: b[h, :, NP:T].rearrange("p g (b t) -> p g b t", t=8),
                              ps[h, 3, 256 * kv:256 * kv + 256].rearrange("p (b g t) -> p g b t", g=4, t=8)))
            return parts

        def unit_source(u):
            kind, l, i = u
            if kind == "mk":
                return A["w_mem_k"][l].rearrange("(k p) n -> p k n", p=P)
            if kind == "mv":
                return A["w_mem_v"][l].rearrange("(k p) n -> p k n", p=P)
            if kind == "z":
                return A["w_in"][l].rearrange("(k p) n -> p k n", p=P)[:, :, Z_COLS[i]:Z_COLS[i] + 256]
            if kind == "pconv":
                return A["p_conv"][l].rearrange("(k p) n -> p k n", p=P)
            if kind == "pmem":
                return A["p_mem"][l].rearrange("(k p) n -> p k n", p=P)
            if kind == "wo":
                return A["w_o"][l].rearrange("(k p) n -> p k n", p=P)[:, :, 256 * i:256 * i + 256]
            if kind == "fg":
                return A["ffn_w_gate"][0].rearrange("(k p) n -> p k n", p=P)[:, :, 256 * i:256 * i + 256]
            if kind == "fu":
                return A["ffn_w_up"][0].rearrange("(k p) n -> p k n", p=P)[:, :, 256 * i:256 * i + 256]
            assert kind == "fd"
            return A["ffn_w_down"][0][256 * i:256 * i + 256, :].rearrange("(k p) n -> p k n", p=P)

        def tiled(buf, width):
            return buf[:, :].rearrange("p (k n) -> p k n", n=width)

        @block.sync
        def _(sp):
            for t in range(2):
                sp.dma_start(mstage[:, t, :], A["mem_prompt"][0, 128 * t:128 * t + 128, :]).then_inc(ld_mem, 16)
            for n, u in enumerate(STREAM):
                if n == 1:
                    for t in range(2):
                        sp.dma_start(xstage[:, t, :], A["x_prompt"][0, 128 * t:128 * t + 128, :]).then_inc(ld_x, 16)
                    sp.dma_start(xstage[0:64, 2, :], A["x_sample"].rearrange("b t d -> (b t) d")).then_inc(ld_x, 16)
                s = n % RING
                if n >= RING:
                    sp.wait_ge(unit_done, n - RING + 1)
                if u[0] == "pattn":
                    rows = A["p_attn"][u[1]].rearrange("(a g d) n -> a d g n", a=2, g=4)
                    for a in range(2):
                        sp.dma_start(tiled(raw[s], 512)[64 * a:64 * a + 64],
                                     rows[a, :, :, 512 * u[2]:512 * u[2] + 512]).then_inc(ld[s], 16)
                else:
                    src = unit_source(u)
                    sp.dma_start(tiled(raw[s], src.shape[2]), src).then_inc(ld[s], 16)

            def expert_unit(step, e, n):
                kind, i = EXPERT[n]
                s = n % RING_MOE
                sp.wait_ge(unit_done, step * NX + (N_DENSE - RING_MOE + n + 1))
                if kind == "d":
                    src = A["exp_w_down"][0][bass.ds(e, 1), 256 * i:256 * i + 256, :]
                    sp.dma_start(tiled(raw_moe[s], D), src.rearrange("o (k p) n -> p (o k) n", p=P)).then_inc(ld[s], 16)
                    return
                rows = slice(0, D // 2) if kind == "a" else slice(D // 2, D)
                for half, name in enumerate(("exp_w_gate", "exp_w_up")):
                    src = A[name][0][bass.ds(e, 1), rows, 256 * i:256 * i + 256]
                    sp.dma_start(tiled(raw_moe[s], 512)[:, :, 256 * half:256 * half + 256],
                                 src.rearrange("o (k p) n -> p (o k) n", p=P)).then_inc(ld[s], 16)

            sp.wait_ge(unit_done, N_DENSE)
            sp.wait_ge(dma_mid, 16 * (8 + 20 * 2))
            with sp.Fori(0, NE - 1) as step:
                for n in range(NX):
                    expert_unit(step, step, n)
            sp.wait_ge(rt_total, 1)
            total = sp.value_load(total_i[0:1, 0:1], min_val=NE, max_val=ROUNDS * NE)
            with sp.Fori(NE - 1, total) as step:
                for n in range(NX):
                    expert_unit(step, step % NE, n)
            for n in range(AHEAD):
                expert_unit(total, 0, n)
            for t, (t0, tn) in enumerate(TILES):
                sp.wait_ge(fin_cp, t + 1)
                sp.wait_ge(fin_cp2, t + 1)
                dst = (O["y_prompt"][0, t0:t0 + tn, :] if t < 2
                       else O["y_sample"].rearrange("b t d -> (b t) d"))
                sp.dma_start(dst, yout[0:tn, t, :]).then_inc(dma_y, 16)
            sp.wait_ge(dma_y, 16 * 3)

        @block.gpsimd
        def _(pool):
            steps = [0]

            def link(ins):
                steps[0] += 1
                ins.then_inc(pchain, 1)
                pool.wait_ge(pchain, steps[0])

            link(pool.memset(ident[:, :], 0.0))
            pool.affine_select(out=ident[:, :], in_=ident[:, :], compare_op=ALU.not_equal, fill=1.0,
                               base=0, pattern=[[-1, P]], channel_multiplier=1).then_inc(const, 1)
            pool.memset(mean_of[:, :], 1.0 / D).then_inc(const, 1)
            link(pool.memset(mask_win[:, :], 0.0))
            pool.affine_select(out=mask_win[:, 0:128], in_=mask_win[:, 0:128], compare_op=ALU.is_gt,
                               fill=NEG, base=0, pattern=[[1, P]], channel_multiplier=-1).then_inc(const, 1)
            pool.affine_select(out=mask_win[:, 128:256], in_=mask_win[:, 128:256], compare_op=ALU.is_ge,
                               fill=NEG, base=0, pattern=[[-1, P]], channel_multiplier=1).then_inc(const, 1)
            pool.memset(eps[:, :], EPS).then_inc(const, 1)
            pool.iota(row_i[:, 0:1], pattern=[[0, 1]], base=0, channel_multiplier=1).then_inc(const, 1)
            pool.iota(iota_i[:, :], pattern=[[1, P]], base=0, channel_multiplier=0).then_inc(const, 1)
            for i, name in enumerate(("ln1_g", "ln1_b", "ln2_g", "ln2_b")):
                pool.dma_start(vstage[16 * i:16 * i + 16, :],
                               A[name].rearrange("l (k p) -> (l k) p", p=P)).then_inc(ld_vec, 16)
            pool.dma_start(vstage[64:76, :], A["conv_w"].rearrange("l w (k p) -> (l w k) p", p=P)).then_inc(ld_vec, 16)

            def load_mem_k(l, g):
                pool.dma_start(kstage[:, :, :, :].rearrange("p b k n -> p (b k) n"),
                               A["cache_mem_k"][l, 4 * g:4 * g + 4].rearrange("b (k p) h d -> p (b k) (h d)", p=P)
                               ).then_inc(ld_memk, 16)

            def load_mem_v(l, g):
                pool.dma_start(mem_v[:, :, :, :].rearrange("p b k n -> p (b k) n"),
                               A["cache_mem_v"][l, 4 * g:4 * g + 4].rearrange("b (k p) h d -> p (b k) (h d)", p=P)
                               ).then_inc(ld_memv, 16)

            load_mem_k(0, 0)
            load_mem_v(0, 0)
            for l in range(2):
                pool.dma_start(sink_p[:, l, :], A["sink"][l:l + 1, :].to_broadcast([P, 8])).then_inc(ld_const, 16)
                for kv in range(2):
                    for b in range(4):
                        pool.dma_start(
                            sink_s[32 * b:32 * b + 32, l, kv:kv + 1],
                            A["sink"][l, 4 * kv:4 * kv + 4].unsqueeze(1).to_broadcast([4, 8]).unsqueeze(2)
                        ).then_inc(ld_const, 16)

            for l in range(2):
                for name, out in (("cache_win_k", "win_k_sample"), ("cache_win_v", "win_v_sample")):
                    pool.dma_start(O[out][l, :, 0:P - TS].rearrange("b j h d -> b (j h d)"),
                                   A[name][l, :, TS:P].rearrange("b j h d -> b (j h d)")).then_inc(dma_out, 16)

            for l in range(2):
                for i, (buf, name) in enumerate(((mtok, "mem_k_prompt"), (mv, "mem_v_prompt"))):
                    pool.wait_ge(mem_cp, 2 * l + i + 1)
                    for t in range(2):
                        pool.dma_start(O[name][l, 0, 128 * t:128 * t + 128].rearrange("m h d -> m (h d)"),
                                       buf[:, l, t, :]).then_inc(dma_mid, 16)

            for l in range(2):
                e0, j0 = l * N_EVENTS, l * NJ
                if l == 0:
                    pool.wait_ge(unit_done, 4)
                else:
                    pool.wait_ge(unit_done, UNIT_OF[("fd", 0, NBLK - 1)] + 1)
                pool.memset(qm_diag[:, :, :, :], 0.0).then_inc(zeroed, 1)
                pool.memset(uext[:, :, :], 0.0).then_inc(zeroed, 1)
                pool.dma_start(ustage[:, :], A["cache_conv"][l].rearrange("b r c -> (b r) c")).then_inc(ld_conv, 16)
                pool.wait_ge(tr_mm, e0 + EVENT_NO[("memk", 0, 1)] + 1)
                load_mem_k(l, 1)
                pool.wait_ge(tr_mm, e0 + EVENT_NO[("memk", 1, 1)] + 1)
                pool.dma_start(wstage[:, :, :], A["cache_win_k"][l].rearrange("b j h d -> j b (h d)")).then_inc(ld_wink, 16)
                pool.wait_ge(pv_mm, j0 + 3)
                load_mem_v(l, 1)
                pool.wait_ge(sc_mm, j0 + 4)
                pool.dma_start(win_v[:, :, :], A["cache_win_v"][l].rearrange("b j h d -> j b (h d)")).then_inc(ld_winv, 16)
                pool.wait_ge(tr_cp, e0 + EVENT_NO[("kvtok", 0, 0)] + 1)
                for i, kind in enumerate("kv"):
                    pool.dma_start(O[f"win_{kind}_prompt"][l, 0].rearrange("j h d -> j (h d)"),
                                   kvtok[:, i, 1, :]).then_inc(dma_mid, 16)
                    for b in range(NB):
                        pool.dma_start(O[f"win_{kind}_sample"][l, b, P - TS:P].rearrange("t h d -> t (h d)"),
                                       kvtok[TS * b:TS * b + TS, i, 2, :]).then_inc(dma_mid, 16)
                pool.wait_ge(tr_cp, e0 + EVENT_NO[("conv", 0, 0)] + 1)
                pool.dma_start(O["conv_prompt"][l, 0], uout[0:2, :]).then_inc(dma_mid, 16)
                pool.dma_start(O["conv_sample"][l].rearrange("b r c -> (b r) c"), uout[2:18, :]).then_inc(dma_mid, 16)
                if l == 0:
                    pool.wait_ge(tr_mm, e0 + EVENT_NO[("wink", 0, 0)] + 1)
                    load_mem_k(1, 0)
                    pool.wait_ge(pv_mm, j0 + 4)
                    load_mem_v(1, 0)
                pool.wait_ge(dma_mid, 16 * (8 + 20 * (l + 1)))
            pool.wait_ge(unit_done, N_DENSE)
            pool.dma_start(rw[:, :, :], A["router_w"][0].rearrange("(k p) e -> p k e", p=P)).then_inc(ld_const, 16)
            pool.dma_start(rb[:, :], A["router_b"][0:1, :].to_broadcast([P, NE])).then_inc(ld_const, 16)
            link(pool.memset(ones[:, :], 1.0))
            pool.affine_select(out=before[:, :], in_=ones[:, :], compare_op=ALU.is_gt, fill=0.0,
                               base=0, pattern=[[1, P]], channel_multiplier=-1).then_inc(const, 1)
            pool.wait_ge(rt_mm, 1)
            pool.wait_ge(xt_mm, 6)
            pool.tensor_scalar(x[:, :, :], x[:, :, :], ALPHA, None, ALU.mult).then_inc(x_scaled, 1)
            pool.wait_ge(dma_mid, 16 * (8 + 20 * 2))
            pool.wait_ge(dma_out, 16 * 4)
        CONSTS = 7
        CONST_LOADS = 18 * 16

        @block.scalar
        def _(act):
            def hi(n):
                if n >= N_DENSE:
                    return
                act.wait_ge(ld[n % RING], LD_VALUE[n])
                if n >= HI_RING:
                    act.wait_ge(unit_done, n - HI_RING + 1)
                act.activation(high[n % HI_RING][:, :], raw[n % RING][:, :], ACT.Copy).then_inc(hi_done, 1)

            def start_part(k):
                act.wait_ge(start_tr, k + 1)
                bank, t, f = START[k]
                t0, tn = TILES[t]
                src = ps[:, bank, :].rearrange("p (f t) -> p f t", t=P)[:, :, 0:tn]
                act.activation((mTh if k < MEM_STARTS else xh)[:, f:f + 4, t0:t0 + tn], src, ACT.Copy).then_inc(start_hi, 1)

            for k in range(MEM_STARTS):
                start_part(k)
            hi(0)
            for k in range(MEM_STARTS, FIRST_STARTS):
                start_part(k)
            hi(1)
            for n in range(4):
                hi(n + AHEAD)
                if n == 0:
                    for k in range(FIRST_STARTS, len(START)):
                        start_part(k)
                if n % 2 == 1:
                    l = n // 2
                    act.wait_ge(mkT_tr, l + 1)
                    act.activation(mkT[:, l, :, :], ps[:, 4 + l, :].rearrange("p (a m) -> p a m", m=256),
                                   ACT.Copy).then_inc(mkT_cp, 1)
            act.wait_ge(const, CONSTS)

            def event_copy(l, e):
                kind, g, r = e
                act.wait_ge(tr_mm, l * N_EVENTS + EVENT_NO[e] + 1)
                if kind == "memk":
                    act.activation(mem_kT[:, 2 * r:2 * r + 2, :, :],
                                   ps_tr[:, :, :].rearrange("p b (a m) -> p b a m", m=256), ACT.Copy).then_inc(tr_cp, 1)
                elif kind == "kvtok":
                    for i in range(2):
                        act.activation(kvtok[:, i, 0:2, :], ps_tr[:, i, 0:256].rearrange("p (t c) -> p t c", c=P), ACT.Copy)
                        act.activation(kvtok[0:64, i, 2, :], ps_tr[0:64, i, 256:384], ACT.Copy)
                    act.wait_ge(zeroed, 2 * l + 2)
                    act.activation(uext[:, :, NP + 2:].rearrange("p f (b t) -> p f b t", t=TS + 2)[:, :, :, 0:2],
                                   ps_tr[:, 0, 384:416].rearrange("p (f b r) -> p f b r", f=2, r=2),
                                   ACT.Copy).then_inc(tr_cp, 1)
                elif kind == "conv":
                    act.activation(uout[:, :], ps_tr[0:18, 0, 0:256], ACT.Copy).then_inc(tr_cp, 1)
                elif kind == "wink":
                    act.activation(win_kT[:, :, :], ps_tr[:, :, :].rearrange("p b (s m) -> p (b s) m", m=P),
                                   ACT.Copy).then_inc(tr_cp, 1)
                else:
                    if l * NJ + g >= 1:
                        act.wait_ge(pv_mm, l * NJ + g)
                    jk, ji = JOBS[g]
                    if jk == "smem":
                        act.activation(pT[:, :, 0:128], ps_tr[:, :, 0:128], ACT.Copy).then_inc(tr_cp, 1)
                    elif jk == "pmem" or (jk == "pwin" and ji[0] == 1):
                        act.activation(pT[:, :, :], ps_tr[:, :, :], ACT.Copy).then_inc(tr_cp, 1)
                    elif jk == "pwin":
                        act.activation(pT[:, 0, :], ps_tr[:, 0, :], ACT.Copy).then_inc(tr_cp, 1)
                    else:
                        act.activation(pT[:, 0, :], ps_tr[:, 0, :], ACT.Copy)
                        act.activation(pT[0:64, 1, :], ps_tr[0:64, 1, :], ACT.Copy).then_inc(tr_cp, 1)

            def exps(l, j):
                kind, idx = JOBS[j]
                n, w = job_shape(kind, idx)
                win = kind in ("pwin", "swin")
                act.wait_ge(sc_cp, l * NJ + j + 1)
                if not win and l * NJ + j >= 1:
                    e = ("probs", (j - 1) % NJ, 0)
                    act.wait_ge(tr_mm, (l if j else l - 1) * N_EVENTS + EVENT_NO[e] + 1)
                if l == 0 and j == 0:
                    act.wait_ge(dma_mid, 8 * 16)
                for g in range(n):
                    src, scale = (sc, 1.0) if win else (ps_sc, SCALE)
                    last = act.activation(sc[:, g, 0:w], src[:, g, 0:w], ACT.Exp, bias=small[:, 8 + g:9 + g],
                                          scale=scale, accum_out=small[:, 16 + g:17 + g])
                if win:
                    last = act.activation(small[:, 24:28], small[:, 12:16], ACT.Exp)
                last.then_inc(exp_done, 1)

            def o_copy(l, j):
                act.wait_ge(pv_mm, l * NJ + j + 1)
                for high_part, _, view, src in attention_out(j):
                    last = act.activation(view(high_part), src, ACT.Copy)
                last.then_inc(o_hi, 1)

            def z_copy(l, f):
                n = l * len(OUTS) + OUT_NO[("z", f)]
                wait_out(act, l, ("z", f))
                src = ps[:, n % 3, 0:T]
                if 2 <= f < 6:
                    for a in range(2):
                        head = 2 * (f - 2) + a
                        kv, g = head // 4, head % 4
                        to, of = slice(64 * kv, 64 * kv + 64), slice(64 * a, 64 * a + 64)
                        act.activation(qT[to, g, :], src[of, 0:NP], ACT.Copy)
                        last = act.activation(qS[to, :, g, :], src[of, NP:T].rearrange("p (b t) -> p b t", t=TS), ACT.Copy)
                elif 6 <= f < 8:
                    last = act.activation(kvT[:, f - 6, :], src, ACT.Copy)
                elif 8 <= f < 14:
                    last = act.activation(hbc[:, f - 8, :], src, ACT.Copy)
                elif f < 2:
                    p = f
                    act.wait_ge(zeroed, 2 * l + 2)
                    act.activation(qmT[:, p, :], src[:, 0:NP], ACT.Copy)
                    for a in range(2):
                        h = slice(64 * a, 64 * a + 64)
                        last = act.activation(qm_diag[h, p, :, (2 * p + a) * 8:(2 * p + a) * 8 + 8],
                                              src[h, NP:T].rearrange("p (b t) -> p b t", t=8), ACT.Copy)
                else:
                    g = (f - 14) % 8
                    if f >= 22:
                        act.wait_ge(merge_done, l * len(MERGES)
                                    + MERGE_NO[("pconv" if f < 30 else "pmem", g)] + 1)
                    last = act.activation(gate[:, g, :], src, ACT.Tanh, scale=0.5)
                last.then_inc(z_cp, 1)

            def layer_norm(L, split, vec):
                sq = sq_last if L == 3 else sq_dense
                if L in (0, 2):
                    act.wait_ge(dma_mid, 16 * (8 + 20 * (L // 2 + 1)))
                act.activation(row_f[:, 2:3], eps[:, 0:1], ACT.Sqrt)
                for f in range(KD):
                    act.wait_ge(centered, KD * L + f + 1)
                    act.activation(sq[:, f, :], x[:, f, :], ACT.Square).then_inc(squared, 1)
                act.wait_ge(var_mm, KD * L + KD)
                act.activation(std[:, :], ps[:, VAR, 0:T], ACT.Sqrt, bias=eps[:, 0:1]).then_inc(std_done, 1)
                for f in range(KD):
                    act.wait_ge(normed, KD * L + f + 1)
                    g, b = vecs[:, vec + f:vec + f + 1], vecs[:, vec + 16 + f:vec + 17 + f]
                    out, done = (xh, xh_done) if split else (x, x_done)
                    act.activation(out[:, f, :], sq[:, f, :], ACT.Identity, scale=g, bias=b).then_inc(done, 1)

            def mixer(l):
                units = layer_units(l)
                for i, u in enumerate(units):
                    n = UNIT_OF[u]
                    hi(n + AHEAD)
                    if u[0] == "z":
                        z_copy(l, 2 * u[2])
                        z_copy(l, 2 * u[2] + 1)
                        if u[2] == 7:
                            act.wait_ge(conv_done, l + 1)
                            act.activation(och[:, :, :], hbc[:, 4:6, :], ACT.Copy).then_inc(och_done, 1)
                    for work in SLOTS.get(i, ()):
                        if work[0] == "pv":
                            o_copy(l, work[1])
                        elif work[0] == "event":
                            event_copy(l, work[1:])
                        else:
                            exps(l, work[1])
                    if u[0] == "pattn":
                        for f in range(4 * u[2], 4 * u[2] + 4):
                            act.wait_ge(merge_done, l * len(MERGES) + MERGE_NO[("pattn", f)] + 1)
                            act.activation(xh[:, f, :], merged[:, f, :], ACT.Copy, scale=0.5).then_inc(mh_done, 1)

            mixer(0)
            layer_norm(0, True, 0)
            for i in range(NBLK):
                for half in range(2):
                    hi(UNIT_OF[("fg" if half == 0 else "fu", 0, i)] + AHEAD)
                    if half == 0 and i >= 1:
                        act.wait_ge(ff_h, i)
                        act.activation(hTh[:, 2 * i - 2:2 * i, :], hfull[:, (i - 1) % 2, :, :], ACT.Copy).then_inc(ff_hi, 1)
                    if half == 1:
                        act.wait_ge(unit_done, UNIT_OF[("fg", 0, i)] + 1)
                        if i >= 2:
                            act.wait_ge(ff_h, i - 1)
                        act.activation(silu[:, i % 2, :, :], ps[:, 4 * (i % 2):4 * (i % 2) + 2, 0:T], ACT.Silu).then_inc(ff_silu, 1)
            act.wait_ge(ff_h, NBLK)
            act.activation(hTh[:, 2 * NBLK - 2:2 * NBLK, :], hfull[:, (NBLK - 1) % 2, :, :], ACT.Copy).then_inc(ff_hi, 1)
            for i in range(NBLK):
                hi(UNIT_OF[("fd", 0, i)] + AHEAD)
            layer_norm(1, True, 32)
            mixer(1)
            layer_norm(2, False, 8)

            def hi_moe(step, n):
                s = n % RING_MOE
                loads = LDX_VALUE[n] if n < NX else LDX_STEP[s] + LDX_VALUE[n - NX]
                act.wait_ge(ld[s], step * LDX_STEP[s] + (LD_BASE[s] + loads))
                act.wait_ge(unit_done, step * NX + (N_DENSE + n - HI_RING + 1))
                for part in HALVES:
                    act.activation(high[(N_DENSE + n) % HI_RING][:, part], raw_moe[s][:, part], ACT.Copy).then_inc(hi_done, 1)

            hi_moe(0, 0)
            for k in range(6):
                tn = TILES[k // 2][1]
                act.wait_ge(xt_mm, k + 1)
                act.activation(xtok[0:tn, k // 2, 512 * (k % 2):512 * (k % 2) + 512], ps[0:tn, XT_BANK[k], :],
                               ACT.Copy).then_inc(xt_cp, 1)
                if k == 2:
                    act.wait_ge(rt_top, 1)
                    act.activation(pair[:, :, 1:2], pair[:, :, 0:1], ACT.Exp).then_inc(rt_exp, 1)
            hi_moe(0, 1)

            def gathered(first, c):
                act.wait_ge(side_mm, first + (c + 1))
                act.activation(xn[:, 2 * c:2 * c + 2, :], ps[:, 6 + c % 2, 0:256].rearrange("p (f s) -> p f s", s=P),
                               ACT.Copy).then_inc(xn_cp, 1)

            def hidden_hi(step, i):
                act.wait_ge(e_tr, step * NBLK + (i + 1))
                act.activation(heh[:, i % 2, :, :], ps[:, 4 + i % 2, 0:256].rearrange("p (f s) -> p f s", s=P),
                               ACT.Copy).then_inc(e_hi, 1)

            for c in range(4):
                gathered(0, c)
            act.wait_ge(xn_cp, 4)
            act.activation(xeh[:, :, :], xn[:, :, :], ACT.Copy).then_inc(xe_ok, 1)
            act.wait_ge(rt_total, 1)
            total = act.value_load(total_i[0:1, 0:1], min_val=NE, max_val=ROUNDS * NE)
            with act.Fori(0, total) as step:
                act.activation(row_f[:, 3:4], eps[:, 0:1], ACT.Silu)
                for n, (kind, i) in enumerate(EXPERT):
                    if (kind, i) == ("d", NBLK - 2):
                        hidden_hi(step, NBLK - 1)
                        act.wait_ge(unit_done, step * NX + (N_DENSE + n))
                        act.wait_ge(xn_cp, step * 4 + 8)
                        act.activation(xeh[:, :, :], xn[:, :, :], ACT.Copy).then_inc(xe_ok, 1)
                    hi_moe(step, n + AHEAD)
                    if kind == "a" and i >= 1:
                        hidden_hi(step, i - 1)
                    if kind == "b":
                        act.wait_ge(unit_done, step * NX + (N_DENSE + n + 1))
                        act.activation(sil[:, i % 2, :], ps[:, 2 + i % 2, 0:256], ACT.Silu).then_inc(e_silu, 1)
                    if n in SIDE and SIDE[n][0] == "gather":
                        if SIDE[n][1] == 0:
                            act.wait_ge(xel_ok, step + 1)
                        gathered(step * 14 + 14, SIDE[n][1])
                    if kind == "d" and i == NBLK - 1:
                        act.wait_ge(unit_done, step * NX + (N_DENSE + NX))
                        act.wait_ge(slot_ok, step + 2)
                        act.activation(ygh[:, :], ps[:, 0:2, :].rearrange("p b n -> p (b n)"), ACT.Copy,
                                       scale=gs_cur[:, 0:1]).then_inc(y_hi, 1)
            layer_norm(3, False, 40)
            for t, (t0, tn) in enumerate(TILES):
                act.wait_ge(fin_tr, 4 + t)
                act.activation(yout[0:tn, t, 512:1024], ps[0:tn, FIN_BANK[2 * t + 1], :], ACT.Copy).then_inc(fin_cp2, 1)

        @block.vector
        def _(dve):
            links = [0]

            def link(ins):
                links[0] += 1
                ins.then_inc(chain, 1)
                dve.wait_ge(chain, links[0])

            def lo(n):
                if n >= N_DENSE:
                    return
                dve.wait_ge(hi_done, n + 1)
                dve.tensor_tensor(low[n % RING][:, :], raw[n % RING][:, :],
                                  high[n % HI_RING][:, :].bitcast(F32), ALU.subtract).then_inc(lo_done, 1)

            def start_part(k):
                bank, t, f = START[k]
                t0, tn = TILES[t]
                src = ps[:, bank, :].rearrange("p (f t) -> p f t", t=P)[:, :, 0:tn]
                high_part, low_part = (mTh, mTl) if k < MEM_STARTS else (xh, xl)
                dve.wait_ge(start_hi, k + 1)
                if k >= MEM_STARTS:
                    dve.tensor_copy(x[:, f:f + 4, t0:t0 + tn], src)
                dve.tensor_tensor(low_part[:, f:f + 4, t0:t0 + tn], src,
                                  high_part[:, f:f + 4, t0:t0 + tn].bitcast(F32), ALU.subtract).then_inc(start_lo, 1)

            for k in range(MEM_STARTS):
                start_part(k)
            lo(0)
            for k in range(MEM_STARTS, FIRST_STARTS):
                start_part(k)
            lo(1)
            for n in range(4):
                lo(n + AHEAD)
                l, is_v = n // 2, n % 2
                dve.wait_ge(unit_done, n + 1)
                dve.tensor_copy((mv if is_v else mtok)[:, l, :, :],
                                ps[:, 3 if n % 2 == 0 else 6, :].rearrange("p (t c) -> p t c", c=256)).then_inc(mem_cp, 1)
                if n == 0:
                    for k in range(FIRST_STARTS, len(START)):
                        start_part(k)
                if n == 3:
                    dve.wait_ge(start_tr, len(START) + 1)
                    dve.tensor_copy(vecs[:, :], ps[:, 2, 0:76]).then_inc(vconst, 1)
            dve.wait_ge(const, CONSTS)
            link(dve.tensor_scalar(row_i[:, 1:2], row_i[:, 0:1], 7, None, ALU.bitwise_and))
            link(dve.tensor_scalar(row_i[:, 2:3], row_i[:, 0:1], 5, None, ALU.logical_shift_right))
            link(dve.tensor_copy(row_f[:, 0:2], row_i[:, 1:3]))
            link(dve.tensor_copy(iota_f[:, :], iota_i[:, :]))
            for bg in range(2):
                first, last_key = row_f[:, 2:3], row_f[:, 3:4]
                link(dve.tensor_scalar(mask_dec[:, bg, 0:128], iota_f[:, :], row_f[:, 0:1], NEG, ALU.is_le, ALU.mult))
                link(dve.tensor_scalar(first, row_f[:, 1:2], 8.0, 32.0 * bg, ALU.mult, ALU.add))
                link(dve.tensor_tensor(last_key, first, row_f[:, 0:1], ALU.add))
                link(dve.tensor_scalar(mask_dec[:, bg, 128:192], iota_f[:, 0:64], first, NEG, ALU.is_lt, ALU.mult))
                link(dve.tensor_scalar(small[:, 0:64], iota_f[:, 0:64], last_key, NEG, ALU.is_gt, ALU.mult))
                link(dve.tensor_tensor(mask_dec[:, bg, 128:192], mask_dec[:, bg, 128:192], small[:, 0:64], ALU.add))
            def scores(l, j):
                kind, idx = JOBS[j]
                n, w = job_shape(kind, idx)
                dve.wait_ge(sc_mm, l * NJ + j + 1)
                if kind in ("smem", "pmem"):
                    if l * NJ + j >= 1:
                        dve.wait_ge(exp_done, l * NJ + j)
                    link(dve.tensor_reduce(small[:, 0:n], ps_sc[:, 0:n, 0:w], AX, ALU.max))
                    dve.tensor_scalar(small[:, 8:8 + n], small[:, 0:n], -SCALE, None, ALU.mult).then_inc(sc_cp, 1)
                    return
                if l * NJ + j >= 1:
                    e = ("probs", (j - 1) % NJ, 0)
                    dve.wait_ge(tr_mm, (l if j else l - 1) * N_EVENTS + EVENT_NO[e] + 1)
                nmax, shift = small[:, 8:8 + n], small[:, 12:12 + n]
                if l == 0 and JOBS[j] == ("pwin", (0, 0)):
                    dve.wait_ge(ld_const, CONST_LOADS)
                    link(dve.tensor_scalar(sink_p[:, :, :], sink_p[:, :, :], -1.0, None, ALU.mult))
                    link(dve.tensor_scalar(sink_s[:, :, :], sink_s[:, :, :], -1.0, None, ALU.mult))
                if kind == "pwin":
                    mask = mask_win[:, 256 - w:256].unsqueeze(1).to_broadcast([P, n, w])
                    nsink = sink_p[:, l, 4 * idx[1]:4 * idx[1] + 4]
                    link(dve.scalar_tensor_tensor(sc[:, 0:n, 0:w], ps_sc[:, 0:n, 0:w], SCALE, mask, ALU.mult, ALU.add))
                else:
                    nsink = sink_s[:, l, :].unsqueeze(2).to_broadcast([P, 2, 2])
                    for kv in range(2):
                        link(dve.scalar_tensor_tensor(sc[:, 2 * kv:2 * kv + 2, 0:w], ps_sc[:, 2 * kv:2 * kv + 2, 0:w],
                                                      SCALE, mask_dec[:, :, :], ALU.mult, ALU.add))
                link(dve.tensor_reduce(small[:, 0:n], sc[:, 0:n, 0:w], AX, ALU.max))
                link(dve.tensor_scalar(small[:, 4:4 + n], small[:, 0:n], -1.0, None, ALU.mult))
                if kind == "swin":
                    v = lambda c: small[:, c:c + 4].rearrange("p (a b) -> p a b", b=2)
                    link(dve.tensor_tensor(v(8), v(4), nsink, ALU.min))
                    dve.tensor_tensor(v(12), v(8), nsink, ALU.subtract).then_inc(sc_cp, 1)
                else:
                    link(dve.tensor_tensor(nmax, small[:, 4:8], nsink, ALU.min))
                    dve.tensor_tensor(shift, nmax, nsink, ALU.subtract).then_inc(sc_cp, 1)

            def normalise(l, j):
                kind, idx = JOBS[j]
                n, w = job_shape(kind, idx)
                dve.wait_ge(exp_done, l * NJ + j + 1)
                den = small[:, 16:16 + n]
                if kind in ("pwin", "swin"):
                    link(dve.tensor_tensor(den, den, small[:, 24:28], ALU.add))
                link(dve.reciprocal(small[:, 20:20 + n], den))
                dve.tensor_tensor(sc[:, 0:n, 0:w], sc[:, 0:n, 0:w],
                                  small[:, 20:20 + n].unsqueeze(2).to_broadcast([P, n, w]), ALU.mult).then_inc(probs, 1)

            def o_low(l, j):
                dve.wait_ge(o_hi, l * NJ + j + 1)
                for bh, bl, view, src in attention_out(j):
                    last = dve.tensor_tensor(view(bl), src, view(bh).bitcast(F32), ALU.subtract)
                last.then_inc(o_lo, 1)

            def conv(l):
                dve.wait_ge(z_cp, l * 38 + 14)
                dve.wait_ge(tr_cp, l * N_EVENTS + EVENT_NO[("kvtok", 0, 0)] + 1)
                dve.wait_ge(const, CONSTS)
                h, b_gate, c_gate = hbc[:, 0:2, :], hbc[:, 2:4, :], hbc[:, 4:6, :]
                smp = lambda s: uext[:, :, NP + 2:].rearrange("p f (b t) -> p f b t", t=TS + 2)[:, :, :, s:s + TS]
                bt = lambda a: a[:, :, NP:T].rearrange("p f (b t) -> p f b t", t=TS)
                link(dve.tensor_tensor(uext[:, :, 2:NP + 2], c_gate[:, :, 0:NP], h[:, :, 0:NP], ALU.mult))
                for f in range(2):
                    link(dve.tensor_tensor(smp(2)[:, f], bt(c_gate)[:, f], bt(h)[:, f], ALU.mult))
                for f in range(2):
                    w = lambda j: vecs[:, 64 + 6 * l + 2 * j + f:65 + 6 * l + 2 * j + f]
                    for out, u in ((c_gate[:, f, 0:NP], lambda s: uext[:, f, s:s + NP]),
                                   (bt(c_gate)[:, f], lambda s: smp(s)[:, f])):
                        link(dve.tensor_scalar(out, u(0), w(0), None, ALU.mult))
                        link(dve.scalar_tensor_tensor(out, u(1), w(1), out, ALU.mult, ALU.add))
                        link(dve.scalar_tensor_tensor(out, u(2), w(2), out, ALU.mult, ALU.add))
                dve.tensor_tensor(c_gate[:, :, :], c_gate[:, :, :], b_gate, ALU.mult).then_inc(conv_done, 1)

            def last_rows(l):
                dve.tensor_copy(ulast[:, :, 0:2], uext[:, :, NP:NP + 2])
                dve.tensor_copy(ulast[:, :, 2:18].rearrange("p f (b r) -> p f b r", r=2),
                                uext[:, :, NP + 2:].rearrange("p f (b t) -> p f b t", t=TS + 2)[:, :, :, TS:TS + 2]
                                ).then_inc(ulast_done, 1)

            def merge(l, kind, f):
                n = l * len(OUTS) + OUT_NO[(kind, f)]
                wait_out(dve, l, (kind, f))
                if kind == "pconv":
                    dve.scalar_tensor_tensor(merged[:, f, :], gate[:, f, :], 1.0, ps[:, n % 3, 0:T],
                                             ALU.add, ALU.mult).then_inc(merge_done, 1)
                else:
                    link(dve.scalar_tensor_tensor(gate[:, f, :], gate[:, f, :], 1.0, ps[:, n % 3, 0:T], ALU.add, ALU.mult))
                    dve.tensor_tensor(merged[:, f, :], merged[:, f, :], gate[:, f, :], ALU.add).then_inc(merge_done, 1)

            def merged_lo(l, f):
                dve.wait_ge(mh_done, KD * l + f + 1)
                dve.scalar_tensor_tensor(xl[:, f, :], merged[:, f, :], 0.5, xh[:, f, :].bitcast(F32),
                                         ALU.mult, ALU.subtract).then_inc(ml_done, 1)

            def residual(l, f):
                n = l * len(OUTS) + OUT_NO[("wo", f)]
                wait_out(dve, l, ("wo", f))
                dve.scalar_tensor_tensor(x[:, f, :], x[:, f, :], ALPHA, ps[:, n % 3, 0:T],
                                         ALU.mult, ALU.add).then_inc(resid, 1)

            def layer_norm(L, vec):
                dve.wait_ge(mean_mm, L + 1)
                for f in range(KD):
                    dve.tensor_tensor(x[:, f, :], x[:, f, :], ps[:, MEAN, 0:T], ALU.subtract).then_inc(centered, 1)
                dve.wait_ge(std_done, L + 1)
                dve.reciprocal(std[:, :], std[:, :]).then_inc(rstd_done, 1)
                dve.wait_ge(rstd_done, L + 1)
                sq = sq_last if L == 3 else sq_dense
                for f in range(KD + 1):
                    if f < KD:
                        dve.tensor_tensor(sq[:, f, :], x[:, f, :], std[:, :], ALU.mult).then_inc(normed, 1)
                    if vec is not None and f >= 1:
                        dve.wait_ge(x_new, KD * L + f)
                        dve.wait_ge(xh_done, KD * L + f)
                        dve.tensor_tensor(xl[:, f - 1, :], x[:, f - 1, :], xh[:, f - 1, :].bitcast(F32),
                                          ALU.subtract).then_inc(xl_done, 1)
                    if vec is not None and f < KD:
                        dve.wait_ge(normed, KD * L + f + 1)
                        dve.tensor_scalar(x[:, f, :], sq[:, f, :], vecs[:, vec + f:vec + f + 1],
                                          vecs[:, vec + 16 + f:vec + 17 + f], ALU.mult, ALU.add).then_inc(x_new, 1)

            def mixer(l):
                pending = None
                for i, u in enumerate(layer_units(l)):
                    if u[0] == "pattn":
                        for f in range(4 * u[2], 4 * u[2] + 4):
                            merge(l, "pattn", f)
                            if f == 1:
                                lo(UNIT_OF[u] + AHEAD)
                            if f % 4 >= 1:
                                merged_lo(l, f - 1)
                        merged_lo(l, 4 * u[2] + 3)
                        if u[2] == 1:
                            lo(UNIT_OF[u] + AHEAD)
                        continue
                    if u[0] in ("pconv", "pmem"):
                        for f in range(KD):
                            merge(l, u[0], f)
                    lo(UNIT_OF[u] + AHEAD)
                    if u == ("z", l, 6):
                        conv(l)
                    if u == ("z", l, 8):
                        dve.wait_ge(och_done, l + 1)
                        dve.tensor_tensor(ocl[:, :, :], hbc[:, 4:6, :], och[:, :, :].bitcast(F32), ALU.subtract).then_inc(ocl_done, 1)
                        dve.wait_ge(ocl_done, l + 1)
                    if u == ("z", l, 6):
                        last_rows(l)
                    if pending is not None:
                        normalise(l, pending)
                        pending = None
                    for work in SLOTS.get(i, ()):
                        if work[0] == "pv":
                            o_low(l, work[1])
                        elif work[0] == "scores":
                            scores(l, work[1])
                            pending = work[1]
                    if u[0] == "wo":
                        residual(l, 2 * u[2])
                        residual(l, 2 * u[2] + 1)

            mixer(0)
            layer_norm(0, 0)

            def ffn_low(i):
                dve.wait_ge(ff_hi, i + 1)
                dve.tensor_tensor(hTl[:, 2 * i:2 * i + 2, :], hfull[:, i % 2, :, :],
                                  hTh[:, 2 * i:2 * i + 2, :].bitcast(F32), ALU.subtract).then_inc(ff_lo, 1)

            for i in range(NBLK):
                lo(UNIT_OF[("fg", 0, i)] + AHEAD)
                if i >= 1:
                    ffn_low(i - 1)
                lo(UNIT_OF[("fu", 0, i)] + AHEAD)
                dve.wait_ge(ff_silu, i + 1)
                dve.wait_ge(unit_done, UNIT_OF[("fu", 0, i)] + 1)
                if i >= 2:
                    dve.wait_ge(ff_lo, i - 1)
                dve.tensor_tensor(hfull[:, i % 2, :, :], silu[:, i % 2, :, :],
                                  ps[:, 4 * (i % 2) + 2:4 * (i % 2) + 4, 0:T], ALU.mult).then_inc(ff_h, 1)
            ffn_low(NBLK - 1)
            for i in range(NBLK):
                lo(UNIT_OF[("fd", 0, i)] + AHEAD)
            for k, f in enumerate((4, 5, 6, 7, 0, 1, 2, 3)):
                if k < KD - 1:
                    dve.wait_ge(down_mm, k + 1)
                else:
                    dve.wait_ge(unit_done, UNIT_OF[("fd", 0, NBLK - 1)] + 1)
                dve.scalar_tensor_tensor(x[:, f, :], x[:, f, :], ALPHA, ps[:, f, 0:T], ALU.mult, ALU.add).then_inc(resid, 1)
            layer_norm(1, 32)
            mixer(1)
            layer_norm(2, None)

            dve.memset(top[:, 2, :], 0.0)
            dve.memset(topi[:, 2, :], 0)
            dve.memset(pos[:, :, :], 1.0e6)
            link(dve.memset(gates[:, :, :], 0.0))
            dve.memset(slot_cur[:, :].bitcast(F32), 0.0).then_inc(slot_ok, 1)
            dve.wait_ge(x_done, KD)
            link(dve.memset(ygh[:, :].bitcast(F32), 0.0))
            dve.memset(ygl[:, :].bitcast(F32), 0.0).then_inc(y_lo, 1)
            dve.wait_ge(ld_const, CONST_LOADS + 32)
            dve.wait_ge(rt_mm, 1)
            for t, (t0, tn) in enumerate(TILES):
                last = dve.tensor_tensor(logit[0:tn, t, :], ps[0:tn, t, 0:8], rb[0:tn, :], ALU.add)
            link(last)
            for t, (t0, tn) in enumerate(TILES):
                last = dve.max(top[0:tn, t, :], logit[0:tn, t, :])
            link(last)
            for t, (t0, tn) in enumerate(TILES):
                last = dve.max_index(topi[0:tn, t, :], top[0:tn, t, :], logit[0:tn, t, :])
            link(last)
            dve.tensor_tensor(pair[:, :, 0:1], top[:, :, 1:2], top[:, :, 0:1], ALU.subtract).then_inc(rt_top, 1)
            link(dve.tensor_copy(topf[:, :, :], topi[:, :, :]))
            experts = iota_f[:, 0:NE].unsqueeze(1).to_broadcast([P, 3, NE])
            wide = lambda a: a.to_broadcast([P, 3, NE])
            dve.tensor_tensor(oh1[:, :, :], experts, wide(topf[:, :, 0:1]), ALU.is_equal)
            link(dve.tensor_tensor(oh2[:, :, :], experts, wide(topf[:, :, 1:2]), ALU.is_equal))
            dve.tensor_tensor(chosen[:, :, :], oh1[:, :, :], oh2[:, :, :], ALU.add).then_inc(rt_sel, 1)
            dve.wait_ge(rt_exp, 1)
            link(dve.tensor_scalar(pair[:, :, 2:3], pair[:, :, 1:2], 1.0, None, ALU.add))
            link(dve.reciprocal(pair[:, :, 2:3], pair[:, :, 2:3]))
            link(dve.tensor_tensor(pair[:, :, 3:4], pair[:, :, 1:2], pair[:, :, 2:3], ALU.mult))
            dve.tensor_tensor(oh1[:, :, :], oh1[:, :, :], wide(pair[:, :, 2:3]), ALU.mult)
            link(dve.tensor_tensor(oh2[:, :, :], oh2[:, :, :], wide(pair[:, :, 3:4]), ALU.mult))
            for k in range(ROUNDS):
                last = dve.tensor_tensor(gates[:, :, NE * k:NE * k + NE], oh1[:, :, :], oh2[:, :, :], ALU.add)
            link(last)
            dve.wait_ge(rt_rank, 1)
            ranks = ps[:, 1, 0:24].rearrange("p (t e) -> p t e", e=NE)
            link(dve.scalar_tensor_tensor(posm[:, :, :], chosen[:, :, :], -65536.0, ranks, ALU.mult, ALU.add))
            for k in range(ROUNDS):
                last = dve.tensor_scalar(pos[:, :, NE * k:NE * k + NE], posm[:, :, :], 65536.0 - 128.0 * k, None, ALU.add)
            link(last)

            def lo_half(step, n, half):
                s, part = n % RING_MOE, HALVES[half]
                dve.wait_ge(hi_done, step * (2 * NX) + (N_DENSE + 2 * n + half + 1))
                dve.tensor_tensor(low_moe[s][:, part], raw_moe[s][:, part],
                                  high[(N_DENSE + n) % HI_RING][:, part].bitcast(F32), ALU.subtract).then_inc(lo_done, 1)

            def one_hot(step):
                for t, (t0, tn) in enumerate(TILES):
                    dve.tensor_scalar(onehot[0:tn, t, :], iota_f[0:tn, :], pos[0:tn, t, bass.ds(step, 1)], None, ALU.is_equal)
                dve.tensor_copy(gcol[:, :].unsqueeze(2), gates[:, :, bass.ds(step, 1)]).then_inc(oh_done, 1)

            def tokens_lo(step):
                dve.wait_ge(xe_ok, step + 1)
                dve.tensor_tensor(xel[:, :, :], xn[:, :, :], xeh[:, :, :].bitcast(F32), ALU.subtract).then_inc(xel_ok, 1)

            def slots_copy(first):
                dve.wait_ge(side_mm, first + 5)
                dve.tensor_copy(slot_next[:, :], ps[:, 6, 0:T]).then_inc(side_cp, 1)
                dve.wait_ge(side_mm, first + 6)
                dve.tensor_copy(gs_next[:, :], ps[:, 7, 0:1]).then_inc(side_cp, 1)

            def add_back(first, tiles):
                for f in tiles:
                    dve.wait_ge(side_mm, first + (f + 1))
                    dve.tensor_tensor(x[:, f, :], x[:, f, :], ps[:, 6 + f % 2, 0:T], ALU.add).then_inc(side_cp, 1)

            def hidden_lo(step, i):
                dve.wait_ge(e_hi, step * NBLK + (i + 1))
                dve.tensor_tensor(hel[:, i % 2, :, :], ps[:, 4 + i % 2, 0:256].rearrange("p (f s) -> p f s", s=P),
                                  heh[:, i % 2, :, :].bitcast(F32), ALU.subtract).then_inc(e_lo, 1)

            one_hot(0)
            lo_half(0, 0, 0)
            lo_half(0, 0, 1)
            link(dve.tensor_reduce(cnt[:, 0:1], ps[:, 1, 24:32], AX, ALU.max))
            link(dve.tensor_scalar(cnt[:, 1:2], cnt[:, 0:1], 128.0, float(NE), ALU.is_gt, ALU.mult))
            link(dve.tensor_scalar(cnt[:, 2:3], cnt[:, 0:1], 256.0, float(NE), ALU.is_gt, ALU.mult))
            link(dve.tensor_tensor(cnt[:, 3:4], cnt[:, 1:2], cnt[:, 2:3], ALU.add))
            link(dve.tensor_scalar(cnt[:, 3:4], cnt[:, 3:4], float(NE), None, ALU.add))
            dve.tensor_copy(total_i[:, :], cnt[:, 3:4]).then_inc(rt_total, 1)
            lo_half(0, 1, 0)
            lo_half(0, 1, 1)
            tokens_lo(0)
            slots_copy(0)
            dve.wait_ge(x_scaled, 1)
            dve.wait_ge(rt_total, 1)
            total = dve.value_load(total_i[0:1, 0:1], min_val=NE, max_val=ROUNDS * NE)
            with dve.Fori(0, total) as step:
                for n, (kind, i) in enumerate(EXPERT):
                    ahead = n + AHEAD
                    if (kind, i) == ("d", NBLK - 2):
                        hidden_lo(step, NBLK - 1)
                        lo_half(step, n + 1, 1)
                        dve.wait_ge(unit_done, step * NX + (N_DENSE + n))
                        tokens_lo(step + 1)
                    if (kind, i) != ("b", NBLK - 1):
                        lo_half(step, ahead, 0)
                    if kind != "b" or 0 < i < NBLK - 1:
                        lo_half(step, ahead, 1)
                    if kind == "a" and i >= 1:
                        hidden_lo(step, i - 1)
                    if kind == "b":
                        dve.wait_ge(e_silu, step * NBLK + (i + 1))
                        dve.tensor_tensor(hf[:, i % 2, :], sil[:, i % 2, :], ps[:, 2 + i % 2, 256:512], ALU.mult).then_inc(e_h, 1)
                        if i == 0:
                            lo_half(step, ahead, 1)
                        if i == NBLK - 1:
                            lo_half(step, ahead, 0)
                        if i == NBLK // 2 - 1:
                            one_hot(step + 1)
                    if n in SIDE:
                        what, arg = SIDE[n]
                        if what == "scatter":
                            add_back(step * 14 + 6, arg)
                            if arg[1] == KD - 1:
                                dve.tensor_copy(slot_cur[:, :], slot_next[:, :])
                                dve.tensor_copy(gs_cur[:, :], gs_next[:, :]).then_inc(slot_ok, 1)
                        elif what == "slots":
                            slots_copy(step * 14 + 14)
                    if kind == "d" and i == NBLK - 1:
                        dve.wait_ge(y_hi, step + 1)
                        dve.scalar_tensor_tensor(ygl[:, :], ps[:, 0:2, :].rearrange("p b n -> p (b n)"), gs_cur[:, 0:1],
                                                 ygh[:, :].bitcast(F32), ALU.mult, ALU.subtract).then_inc(y_lo, 1)
            add_back(total * 14 + 6, range(KD))
            layer_norm(3, None)
            for t, (t0, tn) in enumerate(TILES):
                dve.wait_ge(fin_tr, t + 1)
                dve.tensor_copy(yout[0:tn, t, 0:512], ps[0:tn, FIN_BANK[2 * t], :]).then_inc(fin_cp, 1)

        @block.tensor
        def _(pe):
            def product(out, wh, wl, ah, al, first, last):
                pe.matmul(out, wh, ah, start=first, stop=False)
                pe.matmul(out, wl, ah, start=False, stop=False)
                return pe.matmul(out, wh, al, start=False, stop=last)

            def weights(n):
                pe.wait_ge(lo_done, n + 1)
                return high[n % HI_RING], low[n % RING]

            def start_part(k):
                bank, t, f0 = START[k]
                if k >= FIRST_STARTS:
                    pe.wait_ge(start_lo, k - FIRST_STARTS + 2)
                tn = TILES[t][1]
                stage = mstage if k < MEM_STARTS else xstage
                for f in range(4):
                    last = pe.transpose(ps[:, bank, 128 * f:128 * f + tn],
                                        stage[0:tn, t, 128 * (f0 + f):128 * (f0 + f) + 128], ident[0:tn, 0:tn])
                last.then_inc(start_tr, 1)

            pe.wait_ge(const, 1)
            pe.wait_ge(ld_mem, 2 * 16)
            for k in range(MEM_STARTS):
                start_part(k)
            for n in range(4):
                if n == 0:
                    pe.wait_ge(ld_x, 3 * 16)
                    for k in range(MEM_STARTS, FIRST_STARTS):
                        start_part(k)
                    pe.wait_ge(start_lo, MEM_STARTS)
                wh, wl = weights(n)
                if n >= 2:
                    pe.wait_ge(mem_cp, n - 1)
                bank = 3 if n % 2 == 0 else 6
                for t in range(2):
                    for k in range(KD):
                        c = slice(256 * k, 256 * k + 256)
                        tok = slice(128 * t, 128 * t + 128)
                        out = ps[:, bank, 256 * t:256 * t + 256]
                        pe.matmul(out, mTh[:, k, tok], wh[:, c], start=k == 0, stop=False)
                        pe.matmul(out, mTl[:, k, tok], wh[:, c], start=False, stop=False)
                        last = pe.matmul(out, mTh[:, k, tok], wl[:, c], start=False, stop=k == KD - 1)
                last.then_inc(unit_done, 1)
                if n == 0:
                    for k in range(FIRST_STARTS, len(START)):
                        start_part(k)
                if n == 3:
                    pe.wait_ge(ld_vec, 5 * 16)
                    pe.wait_ge(start_lo, MEM_STARTS + 1)
                    pe.transpose(ps[:, 2, 0:76], vstage[:, :], ident[0:76, 0:76]).then_inc(start_tr, 1)
                if n % 2 == 1:
                    l = n // 2
                    pe.wait_ge(mem_cp, 2 * l + 1)
                    pe.wait_ge(start_lo, len(START))
                    for p in range(2):
                        for t in range(2):
                            last = pe.transpose(ps[:, 4 + l, 256 * p + 128 * t:256 * p + 128 * t + 128],
                                                mtok[:, l, t, 128 * p:128 * p + 128], ident[:, :])
                    last.then_inc(mkT_tr, 1)

            def event(l, e):
                kind, g, r = e
                no = l * N_EVENTS + EVENT_NO[e]
                if no >= 1:
                    pe.wait_ge(tr_cp, no)
                if kind == "memk":
                    if r == 0:
                        pe.wait_ge(ld_memk, 16 * (2 * l + g + 1))
                    for b in range(2):
                        for p in range(2):
                            for t in range(2):
                                last = pe.transpose(ps_tr[:, b, 256 * p + 128 * t:256 * p + 128 * t + 128],
                                                    kstage[:, 2 * r + b, t, 128 * p:128 * p + 128], ident[:, :])
                elif kind == "kvtok":
                    pe.wait_ge(z_cp, l * 38 + 8)
                    pe.wait_ge(ld_conv, 16 * (l + 1))
                    for i in range(2):
                        for t, (t0, tn) in enumerate(TILES):
                            pe.transpose(ps_tr[0:tn, i, 128 * t:128 * t + 128], kvT[:, i, t0:t0 + tn], ident[:, :])
                    for f in range(2):
                        last = pe.transpose(ps_tr[:, 0, 384 + 16 * f:400 + 16 * f],
                                            ustage[0:16, 128 * f:128 * f + 128], ident[0:16, 0:16])
                elif kind == "conv":
                    pe.wait_ge(ulast_done, l + 1)
                    for f in range(2):
                        last = pe.transpose(ps_tr[0:18, 0, 128 * f:128 * f + 128], ulast[:, f, :], ident[:, :])
                elif kind == "wink":
                    pe.wait_ge(ld_wink, 16 * (l + 1))
                    for b in range(NB):
                        last = pe.transpose(ps_tr[:, b // 4, 128 * (b % 4):128 * (b % 4) + 128], wstage[:, b, :], ident[:, :])
                else:
                    pe.wait_ge(probs, l * NJ + g + 1)
                    jk, ji = JOBS[g]
                    n, w = job_shape(jk, ji)
                    for s in range(n):
                        if jk == "swin":
                            pe.transpose(ps_tr[:, 0, 128 * s:128 * s + 128], sc[:, s, 0:128], ident[:, :])
                            last = pe.transpose(ps_tr[0:64, 1, 128 * s:128 * s + 128], sc[:, s, 128:192], ident[:, :])
                        else:
                            for kb in range(w // 128):
                                last = pe.transpose(ps_tr[:, kb, 128 * s:128 * s + 128],
                                                    sc[:, s, 128 * kb:128 * kb + 128], ident[:, :])
                last.then_inc(tr_mm, 1)

            def scores(l, j):
                kind, idx = JOBS[j]
                if l * NJ + j >= 1:
                    pe.wait_ge(exp_done, l * NJ + j)
                if j == 0:
                    pe.wait_ge(z_cp, l * 38 + 2)
                if kind == "smem":
                    pe.wait_ge(tr_cp, l * N_EVENTS + EVENT_NO[("memk", idx, 1)] + 1)
                    for b in range(4):
                        for p in range(2):
                            last = pe.matmul(ps_sc[32 * b:32 * b + 32, 0, :], qm_diag[:, p, 4 * idx + b, :],
                                             mem_kT[:, b, p, :], start=p == 0, stop=p == 1)
                elif kind == "pmem":
                    pe.wait_ge(mkT_cp, l + 1)
                    for s, h in enumerate(SEGMENT_HEADS):
                        r = slice(64 * (h % 2), 64 * (h % 2) + 64)
                        last = pe.matmul(ps_sc[:, s, :], qmT[r, h // 2, 128 * idx:128 * idx + 128],
                                         mkT[r, l, h // 2, :], start=True, stop=True)
                elif kind == "pwin":
                    n, kv = idx
                    r = slice(64 * kv, 64 * kv + 64)
                    for g in range(4):
                        last = pe.matmul(ps_sc[:, g, 0:128 * (n + 1)], qT[r, g, 128 * n:128 * n + 128],
                                         kvT[r, 0, 0:128 * (n + 1)], start=True, stop=True)
                else:
                    pe.wait_ge(tr_cp, l * N_EVENTS + EVENT_NO[("wink", 0, 0)] + 1)
                    for kv in range(2):
                        r = slice(64 * kv, 64 * kv + 64)
                        for bg in range(2):
                            for b in range(4):
                                seq = 4 * bg + b
                                q = qS[r, seq, :, :].rearrange("p g t -> p (g t)")
                                out = ps_sc[32 * b:32 * b + 32, 2 * kv + bg, :]
                                pe.matmul(out[:, 0:128], q, win_kT[r, seq, :], start=True, stop=True)
                                last = pe.matmul(out[:, 128:192], q, kvT[r, 0, NP:T], start=True, stop=True)
                last.then_inc(sc_mm, 1)

            def values(l, j):
                kind, idx = JOBS[j]
                pe.wait_ge(tr_cp, l * N_EVENTS + EVENT_NO[("probs", j, 0)] + 1)
                if l * NJ + j >= 1:
                    pe.wait_ge(o_lo, l * NJ + j)
                if kind == "smem":
                    pe.wait_ge(ld_memv, 16 * (2 * l + idx + 1))
                    for b in range(4):
                        for p in range(2):
                            c = 128 * p + 32 * b
                            for t in range(2):
                                last = pe.matmul(ps[:, 3, c:c + 32], mem_v[:, b, t, 128 * p:128 * p + 128],
                                                 pT[:, t, 32 * b:32 * b + 32], start=t == 0, stop=t == 1)
                elif kind == "pmem":
                    pe.wait_ge(mem_cp, 2 * l + 2)
                    for s, h in enumerate(SEGMENT_HEADS):
                        out = ps[64 * (h % 2):64 * (h % 2) + 64, 3, 128 * (h // 2):128 * (h // 2) + 128]
                        for t in range(2):
                            last = pe.matmul(out, mv[:, l, t, 64 * h:64 * h + 64], pT[:, t, 128 * s:128 * s + 128],
                                             start=t == 0, stop=t == 1)
                elif kind == "pwin":
                    n, kv = idx
                    for t in range(n + 1):
                        last = pe.matmul(ps[64 * kv:64 * kv + 64, 3, :], kvtok[:, 1, t, 64 * kv:64 * kv + 64],
                                         pT[:, t, :], start=t == 0, stop=t == n)
                else:
                    pe.wait_ge(ld_winv, 16 * (l + 1))
                    pe.matmul(ps[:, 3, :], kvtok[0:64, 1, 2, :], pT[0:64, 1, :], start=True, stop=False)
                    out = ps[:, 3, :].rearrange("p (v c) -> p v c", c=256)
                    cached = pT[:, 0, :].rearrange("p (v c) -> p v c", c=256)
                    for b in range(NB):
                        last = pe.matmul(out[:, :, 32 * b:32 * b + 32], win_v[:, b, :], cached[:, :, 32 * b:32 * b + 32],
                                         start=False, stop=b == NB - 1)
                last.then_inc(pv_mm, 1)

            def free_bank(l, q):
                if q < 3:
                    return
                kind, f = OUTS[q - 3]
                if kind == "z":
                    pe.wait_ge(z_cp, l * 38 + f + 1)
                elif kind == "wo":
                    pe.wait_ge(resid, 16 * l + f + 1)
                else:
                    pe.wait_ge(merge_done, l * len(MERGES) + MERGE_NO[(kind, f)] + 1)

            def mixer(l):
                for i, u in enumerate(layer_units(l)):
                    n = UNIT_OF[u]
                    wh, wl = weights(n)
                    if u[0] in ("z", "wo"):
                        tiles, kn, width = [(u[0], 2 * u[2]), (u[0], 2 * u[2] + 1)], KD, 256
                        ah, al = xh, xl
                    elif u[0] == "pattn":
                        tiles, kn, width = [("pattn", 4 * u[2] + f) for f in range(4)], 4, 512
                        ah, al = oah, oal
                        pe.wait_ge(o_lo, l * NJ + NJ)
                    else:
                        tiles, kn, width = [(u[0], f) for f in range(KD)], 2, D
                        ah, al = (och, ocl) if u[0] == "pconv" else (omh, oml)
                        if u[0] == "pconv":
                            pe.wait_ge(ocl_done, l + 1)
                        else:
                            pe.wait_ge(o_lo, l * NJ + 4)
                    side_by_side = i == 0 or u == ("wo", l, 0)
                    if side_by_side:
                        qs = [OUT_NO[tile] for tile in tiles]
                        for k in range(KD):
                            if i == 0 and l == 1:
                                pe.wait_ge(xl_done, KD + k + 1)
                            if i > 0:
                                pe.wait_ge(ml_done, KD * l + k + 1)
                            for m in range(2):
                                if k == 0:
                                    free_bank(l, qs[m])
                                c = slice(256 * k + 128 * m, 256 * k + 128 * m + 128)
                                last = product(ps[:, (l * len(OUTS) + qs[m]) % 3, 0:T], wh[:, c], wl[:, c],
                                               xh[:, k, :], xl[:, k, :], k == 0, k == KD - 1)
                                if m == 0 and k == KD - 1:
                                    last.then_inc(out_mm, 1)
                    for m, tile in enumerate(() if side_by_side else tiles):
                        q = OUT_NO[tile]
                        free_bank(l, q)
                        for k in range(kn):
                            c = slice(width * k + 128 * m, width * k + 128 * m + 128)
                            last = product(ps[:, (l * len(OUTS) + q) % 3, 0:T], wh[:, c], wl[:, c],
                                           ah[:, k, :], al[:, k, :], k == 0, k == kn - 1)
                        if m < len(tiles) - 1:
                            last.then_inc(out_mm, 1)
                    last.then_inc(unit_done, 1)
                    for work in SLOTS.get(i, ()):
                        if work[0] == "pv":
                            values(l, work[1])
                        elif work[0] == "event":
                            event(l, work[1:])
                        else:
                            scores(l, work[1])

            def mean_tile(f, first, last):
                return pe.matmul(ps[:, MEAN, 0:T], mean_of[:, :], x[:, f, :], start=first, stop=last)

            def variance(L):
                sq = sq_last if L == 3 else sq_dense
                for f in range(KD):
                    pe.wait_ge(squared, KD * L + f + 1)
                    pe.matmul(ps[:, VAR, 0:T], mean_of[:, :], sq[:, f, :], start=f == 0, stop=f == KD - 1
                              ).then_inc(var_mm, 1)

            def layer_norm(L, order):
                for k, f in enumerate(order):
                    pe.wait_ge(resid, KD * L + k + 1)
                    last = mean_tile(f, k == 0, k == KD - 1)
                last.then_inc(mean_mm, 1)
                variance(L)

            DOWN = (4, 5, 6, 7, 0, 1, 2, 3)
            pe.wait_ge(vconst, 1)
            pe.wait_ge(const, CONSTS)
            mixer(0)
            layer_norm(0, range(KD))
            for i in range(NBLK):
                for half, kind in enumerate(("fg", "fu")):
                    n = UNIT_OF[(kind, 0, i)]
                    wh, wl = weights(n)
                    if i >= 2 and half == 0:
                        pe.wait_ge(ff_h, i - 1)
                    order = [(m, k) for m in range(2) for k in range(KD)]
                    if i == 0 and half == 0:
                        order.sort(key=lambda mk: mk[1])
                    for m, k in order:
                        if i == 0 and half == 0 and m == 0:
                            pe.wait_ge(xl_done, k + 1)
                        c = slice(256 * k + 128 * m, 256 * k + 128 * m + 128)
                        last = product(ps[:, 4 * (i % 2) + 2 * half + m, 0:T], wh[:, c], wl[:, c],
                                       xh[:, k, :], xl[:, k, :], k == 0, k == KD - 1)
                    last.then_inc(unit_done, 1)
            for i in range(NBLK):
                n = UNIT_OF[("fd", 0, i)]
                wh, wl = weights(n)
                pe.wait_ge(ff_lo, i + 1)
                for k in range(2):
                    for f in DOWN:
                        if i == 0 and k == 0 and f in (4, 0):
                            pe.wait_ge(ff_h, NBLK - 1 if f == 4 else NBLK)
                        c = slice(D * k + 128 * f, D * k + 128 * f + 128)
                        last = product(ps[:, f, 0:T], wh[:, c], wl[:, c], hTh[:, 2 * i + k, :], hTl[:, 2 * i + k, :],
                                       i == 0 and k == 0, i == NBLK - 1 and k == 1)
                        if i == NBLK - 1 and k == 1 and f != DOWN[-1]:
                            last.then_inc(down_mm, 1)
                last.then_inc(unit_done, 1)
            layer_norm(1, DOWN)
            mixer(1)
            layer_norm(2, range(KD))

            pe.wait_ge(ld_const, CONST_LOADS + 32)
            for k in range(KD):
                pe.wait_ge(x_done, k + 1)
                for t, (t0, tn) in enumerate(TILES):
                    last = pe.matmul(ps[0:tn, t, 0:8], x[:, k, t0:t0 + tn], rw[:, k, :], start=k == 0, stop=k == KD - 1)
            last.then_inc(rt_mm, 1)

            def token_major(k):
                t0, tn = TILES[k // 2]
                for f in range(4):
                    last = pe.transpose(ps[0:tn, XT_BANK[k], 128 * f:128 * f + 128], x[:, 4 * (k % 2) + f, t0:t0 + tn], ident[:, :])
                last.then_inc(xt_mm, 1)

            for k in range(3):
                token_major(k)
            pe.wait_ge(rt_sel, 1)
            pe.wait_ge(const, CONSTS + 1)
            for t, (t0, tn) in enumerate(TILES):
                for m in range(t):
                    pe.matmul(ps[:, 1, 8 * t:8 * t + 8], ones[:, :], chosen[:, m, :], start=m == 0, stop=False)
                pe.matmul(ps[:, 1, 8 * t:8 * t + 8], before[0:tn, :], chosen[0:tn, t, :], start=t == 0, stop=True)
            for t, (t0, tn) in enumerate(TILES):
                last = pe.matmul(ps[:, 1, 24:32], ones[0:tn, :], chosen[0:tn, t, :], start=t == 0, stop=t == 2)
            last.then_inc(rt_rank, 1)
            for k in range(3, 6):
                if k == 5:
                    pe.wait_ge(xt_cp, 1)
                token_major(k)

            def gather(chunks, scattered, c):
                if c >= 2:
                    pe.wait_ge(xn_cp, chunks + (c - 1))
                elif scattered is not None:
                    pe.wait_ge(side_cp, scattered + (c + 7))
                for f in range(2):
                    out = ps[:, 6 + c % 2, 128 * f:128 * f + 128]
                    for t, (t0, tn) in enumerate(TILES):
                        cols = slice(128 * (2 * c + f), 128 * (2 * c + f) + 128)
                        last = pe.matmul(out, xtok[0:tn, t, cols], onehot[0:tn, t, :], start=t == 0, stop=t == 2)
                last.then_inc(side_mm, 1)

            def slots_and_gates(chunks):
                pe.wait_ge(xn_cp, chunks + 3)
                for t, (t0, tn) in enumerate(TILES):
                    last = pe.transpose(ps[:, 6, t0:t0 + tn], onehot[0:tn, t, :], ident[0:tn, 0:tn])
                last.then_inc(side_mm, 1)
                pe.wait_ge(xn_cp, chunks + 4)
                for t, (t0, tn) in enumerate(TILES):
                    last = pe.matmul(ps[:, 7, 0:1], onehot[0:tn, t, :], gcol[0:tn, t:t + 1], start=t == 0, stop=t == 2)
                last.then_inc(side_mm, 1)

            def scatter(first, f):
                pe.wait_ge(side_cp, first + (f - 1))
                cols = slice(128 * f, 128 * f + 128)
                out = ps[:, 6 + f % 2, 0:T]
                pe.matmul(out, ygh[:, cols], slot_cur[:, :], start=True, stop=False)
                pe.matmul(out, ygl[:, cols], slot_cur[:, :], start=False, stop=True).then_inc(side_mm, 1)

            pe.wait_ge(xt_cp, 6)
            pe.wait_ge(oh_done, 1)
            for c in range(4):
                gather(0, None, c)
            slots_and_gates(0)
            pe.wait_ge(rt_total, 1)
            total = pe.value_load(total_i[0:1, 0:1], min_val=NE, max_val=ROUNDS * NE)
            with pe.Fori(0, total) as step:
                def block_transposed(i):
                    pe.wait_ge(e_h, step * NBLK + (i + 1))
                    for f in range(2):
                        last = pe.transpose(ps[:, 4 + i % 2, 128 * f:128 * f + 128], hf[:, i % 2, 128 * f:128 * f + 128], ident[:, :])
                    last.then_inc(e_tr, 1)

                for n, (kind, i) in enumerate(EXPERT):
                    def half_there(half):
                        pe.wait_ge(lo_done, step * (2 * NX) + (N_DENSE + 2 * n + half + 1))

                    half_there(0)
                    wh, wl = high[(N_DENSE + n) % HI_RING], low_moe[n % RING_MOE]
                    if kind == "d":
                        pe.wait_ge(e_lo, step * NBLK + (i + 1))
                        if i == 0:
                            pe.wait_ge(y_lo, step + 1)
                        for k in range(2):
                            if k == 1 and i == NBLK - 2:
                                block_transposed(NBLK - 1)
                            if k == 1:
                                half_there(1)
                            for half in range(2):
                                c = slice(D * k + 512 * half, D * k + 512 * half + 512)
                                out = ps[:, half, :]
                                pe.matmul(out, heh[:, i % 2, k, :], wh[:, c], start=i == 0 and k == 0, stop=False)
                                pe.matmul(out, heh[:, i % 2, k, :], wl[:, c], start=False, stop=False)
                                last = pe.matmul(out, hel[:, i % 2, k, :], wh[:, c], start=False,
                                                 stop=i == NBLK - 1 and k == 1)
                        last.then_inc(unit_done, 1)
                        continue
                    if kind == "a":
                        if i == 0:
                            pe.wait_ge(xe_ok, step + 1)
                            pe.wait_ge(xel_ok, step + 1)
                        if i >= 2:
                            pe.wait_ge(e_h, step * NBLK + (i - 1))
                    k0 = 0 if kind == "a" else KD // 2
                    for k in range(KD // 2):
                        if k == KD // 4:
                            half_there(1)
                        c = slice(512 * k, 512 * k + 512)
                        pe.matmul(ps[:, 2 + i % 2, :], xeh[:, k0 + k, :], wh[:, c], start=k0 + k == 0, stop=False)
                        pe.matmul(ps[:, 2 + i % 2, :], xeh[:, k0 + k, :], wl[:, c], start=False, stop=False)
                        last = pe.matmul(ps[:, 2 + i % 2, :], xel[:, k0 + k, :], wh[:, c], start=False, stop=k0 + k == KD - 1)
                    last.then_inc(unit_done, 1)
                    if kind == "a" and i >= 1:
                        block_transposed(i - 1)
                    if n in SIDE:
                        what, arg = SIDE[n]
                        if what == "scatter":
                            if arg[0] == 0:
                                pe.wait_ge(slot_ok, step + 1)
                                pe.wait_ge(y_lo, step + 1)
                            for f in arg:
                                scatter(step * 10 + 2, f)
                        elif what == "gather":
                            if arg == 0:
                                pe.wait_ge(oh_done, step + 2)
                            gather(step * 4 + 4, step * 10 + 2, arg)
                        else:
                            slots_and_gates(step * 4 + 4)
            pe.wait_ge(slot_ok, total + 1)
            pe.wait_ge(y_lo, total + 1)
            for f in range(KD + 1):
                if f < KD:
                    scatter(total * 10 + 2, f)
                if f >= 1:
                    pe.wait_ge(side_cp, total * 10 + (f + 2))
                    last = mean_tile(f - 1, f == 1, f == KD)
            last.then_inc(mean_mm, 1)
            variance(3)
            for half in range(2):
                pe.wait_ge(x_done, KD + 4 * half + 4)
                for t, (t0, tn) in enumerate(TILES):
                    for f in range(4):
                        last = pe.transpose(ps[0:tn, FIN_BANK[2 * t + half], 128 * f:128 * f + 128],
                                            x[:, 4 * half + f, t0:t0 + tn], ident[:, :])
                    last.then_inc(fin_tr, 1)


_INS = ["x_prompt", "x_sample", "mem_prompt", "cache_win_k", "cache_win_v", "cache_conv", "cache_mem_k",
        "cache_mem_v", "w_in", "conv_w", "sink", "p_attn", "p_conv", "p_mem", "w_o", "w_mem_k", "w_mem_v",
        "ln1_g", "ln1_b", "ln2_g", "ln2_b", "ffn_w_gate", "ffn_w_up", "ffn_w_down", "router_w", "router_b",
        "exp_w_gate", "exp_w_up", "exp_w_down"]
_OUTS = [("y_prompt", (1, 256, 1024)), ("y_sample", (8, 8, 1024)),
         ("win_k_prompt", (2, 1, 128, 2, 64)), ("win_v_prompt", (2, 1, 128, 2, 64)),
         ("conv_prompt", (2, 1, 2, 256)),
         ("mem_k_prompt", (2, 1, 256, 4, 64)), ("mem_v_prompt", (2, 1, 256, 4, 64)),
         ("win_k_sample", (2, 8, 128, 2, 64)), ("win_v_sample", (2, 8, 128, 2, 64)),
         ("conv_sample", (2, 8, 2, 256))]


def kernel(**inputs):
    import numpy as _np
    import concourse.bacc as _bacc
    from concourse import mybir as _mybir
    from concourse.bass_utils import run_bass_kernel_spmd as _run

    nc = _bacc.Bacc("TRN2", target_bir_lowering=False, num_devices=1)
    arrays, A, O = {}, {}, {}
    for name in _INS:
        a = _np.ascontiguousarray(inputs[name])
        arrays[f"in_{name}_dram"] = a
        A[name] = nc.dram_tensor(f"in_{name}_dram", a.shape, _mybir.dt.from_np(a.dtype), kind="ExternalInput").ap()
    for name, shape in _OUTS:
        O[name] = nc.dram_tensor(f"out_{name}_dram", shape, _mybir.dt.float32, kind="ExternalOutput").ap()
    build_trunk(nc, A, O)
    r = _run(nc, [arrays], core_ids=[0])
    return tuple(r.results[0][f"out_{name}_dram"] for name, _ in _OUTS)
```
